# Optimizing a Trainium2 kernel written in Bass

```python
import math
import jax, jax.numpy as jnp
from jax import lax
import numpy as np

D_MODEL = 1024
BATCH = 1
SEQ = 512
DEPTH = 1

GRID_W = 64
CTX_LEN = 256
SSD_HEADS = 8
SSD_HEAD_DIM = 64
SSD_INNER = SSD_HEADS * SSD_HEAD_DIM
SSD_STATE = 64
SSD_GROUPS = 2
SSD_CONV = 5
SSD_XBC = SSD_INNER + 2 * SSD_GROUPS * SSD_STATE
SSD_COLS = SSD_INNER + SSD_XBC + 2 * SSD_HEADS
HG_HEADS = 4
HG_DK = 128
HG_DV = 128
HG_INNER = HG_HEADS * HG_DV
HG_COLS = 5 * HG_INNER
D_MIX = SSD_INNER + HG_INNER
IN_COLS = SSD_COLS + HG_COLS
CHUNK = 64
N_EXPERTS = 32
TOP_K = 4
D_FF = D_MODEL
SWIGLU_ALPHA = 1.702
SWIGLU_LIMIT = 7.0
MOE_BLOCK = 128
EPS = 1e-6

kernel_name = 'hybrid_ssd_hgrn2_moe_diffusion_block'

def rmsnorm(x, w):
    xf = x.astype(jnp.float32)
    y = xf * lax.rsqrt(jnp.mean(xf * xf, axis=-1, keepdims=True) + EPS)
    return (y * w.astype(jnp.float32)).astype(x.dtype)

def modulate(h, shift, scale):
    return h * (1 + scale) + shift

def centred_dwconv(x, w, b):
    pad = SSD_CONV // 2
    y = lax.conv_general_dilated(x, w[:, None, :].astype(x.dtype), window_strides=(1,),
                                 padding=[(pad, pad)], dimension_numbers=('NWC', 'WIO', 'NWC'),
                                 feature_group_count=x.shape[-1])
    return y + b

def chunked_scan(q, k, v, log_a, s0):
    bsz, t_len, n_h, _ = q.shape
    n_chunks = t_len // CHUNK
    scalar_decay = log_a.shape[-1] == 1
    causal = jnp.tril(jnp.ones((CHUNK, CHUNK), dtype=bool))[None, None, :, :, None]

    def to_chunks(a):
        a = a.astype(jnp.float32).reshape(bsz, n_chunks, CHUNK, n_h, a.shape[-1])
        return jnp.moveaxis(a, 1, 0)

    def step(s, blk):
        qc, kc, vc, lac = blk
        g = jnp.cumsum(lac, axis=1)
        gh = jnp.swapaxes(g, 1, 2)
        decay = jnp.exp(jnp.where(causal, gh[:, :, :, None, :] - gh[:, :, None, :, :], -jnp.inf))
        if scalar_decay:
            scores = jnp.einsum('bihk,bjhk->bhij', qc, kc) * decay[..., 0]
        else:
            scores = jnp.einsum('bihk,bjhk,bhijk->bhij', qc, kc, decay)
        o = jnp.einsum('bhij,bjhv->bihv', scores, vc) + jnp.einsum('bihk,bhkv->bihv', qc * jnp.exp(g), s)
        g_last = g[:, -1]
        s = jnp.exp(g_last)[..., None] * s + jnp.einsum('bjhk,bjhv->bhkv', kc * jnp.exp(g_last[:, None] - g), vc)
        return s, o

    s_fin, o = lax.scan(step, s0.astype(jnp.float32),
                        (to_chunks(q), to_chunks(k), to_chunks(v), to_chunks(log_a)))
    o = jnp.moveaxis(o, 0, 1).reshape(bsz, t_len, n_h, v.shape[-1])
    return o.astype(v.dtype), s_fin

def bidir_scan(q, k_f, k_b, v, la_f, la_b, s0_f, s0_b):
    rev = lambda a: jnp.flip(a, axis=1)
    o_f, s_f = chunked_scan(q, k_f, v, la_f, s0_f)
    o_b, s_b = chunked_scan(rev(q), rev(k_b), rev(v), rev(la_b), s0_b)
    return o_f + rev(o_b), s_f, s_b

def ssd_branch(u, conv_w, conv_b, dt_bias, a_log, d_skip, norm_w, s0_f, s0_b, need_out):
    bsz, t_len, _ = u.shape
    z = u[..., :SSD_INNER]
    xbc = jax.nn.silu(centred_dwconv(u[..., SSD_INNER:SSD_INNER + SSD_XBC], conv_w, conv_b))
    dt_raw = u[..., SSD_INNER + SSD_XBC:]
    xs = xbc[..., :SSD_INNER].reshape(bsz, t_len, SSD_HEADS, SSD_HEAD_DIM)
    rep = SSD_HEADS // SSD_GROUPS
    gn = SSD_GROUPS * SSD_STATE
    b_mat = jnp.repeat(xbc[..., SSD_INNER:SSD_INNER + gn].reshape(bsz, t_len, SSD_GROUPS, SSD_STATE), rep, axis=2)
    c_mat = jnp.repeat(xbc[..., SSD_INNER + gn:].reshape(bsz, t_len, SSD_GROUPS, SSD_STATE), rep, axis=2)
    dt = jax.nn.softplus(dt_raw.astype(jnp.float32).reshape(bsz, t_len, 2, SSD_HEADS) + dt_bias)
    log_a = dt * (-jnp.exp(a_log.astype(jnp.float32)))
    y, s_f, s_b = bidir_scan(c_mat, b_mat * dt[:, :, 0, :, None], b_mat * dt[:, :, 1, :, None], xs,
                             log_a[:, :, 0, :, None], log_a[:, :, 1, :, None], s0_f, s0_b)
    if not need_out:
        return None, s_f, s_b
    y = (y + d_skip[:, None] * xs).reshape(bsz, t_len, SSD_INNER)
    return rmsnorm(y * jax.nn.silu(z), norm_w), s_f, s_b

def hgrn_branch(u, lb_f, lb_b, norm_w, s0_f, s0_b, need_out):
    bsz, t_len, _ = u.shape
    q, f_raw_f, f_raw_b, i, g = jnp.split(u, 5, axis=-1)
    shape4 = (bsz, t_len, HG_HEADS, HG_DK)
    q = (jax.nn.silu(q) * HG_DK ** -0.5).reshape(shape4)

    def forget(f_raw, lb):
        return (lb + (1 - lb) * jax.nn.sigmoid(f_raw.astype(jnp.float32))).reshape(shape4)

    f_f = forget(f_raw_f, lb_f)
    f_b = forget(f_raw_b, lb_b)
    o, s_f, s_b = bidir_scan(q, 1 - f_f, 1 - f_b, i.reshape(bsz, t_len, HG_HEADS, HG_DV),
                             jnp.log(f_f), jnp.log(f_b), s0_f, s0_b)
    if not need_out:
        return None, s_f, s_b
    o = rmsnorm(o, norm_w.reshape(HG_HEADS, HG_DV)).reshape(bsz, t_len, HG_INNER)
    return o * jax.nn.silu(g), s_f, s_b

def to_col_major(a):
    bsz, t_len, ch = a.shape
    rows = t_len // GRID_W
    return a.reshape(bsz, rows, GRID_W, ch).transpose(0, 2, 1, 3).reshape(bsz, t_len, ch)

def from_col_major(a):
    bsz, t_len, ch = a.shape
    rows = t_len // GRID_W
    return a.reshape(bsz, GRID_W, rows, ch).transpose(0, 2, 1, 3).reshape(bsz, t_len, ch)

def moe_ffn(h, router_w, router_b, w1, b1, w2, b2):
    n_tok, d = h.shape
    n_pairs = n_tok * TOP_K
    logits = h.astype(jnp.float32) @ router_w.astype(jnp.float32) + router_b.astype(jnp.float32)
    top_v, top_i = lax.top_k(logits, TOP_K)
    gates = jax.nn.softmax(top_v, axis=-1)
    flat_e = top_i.reshape(-1)
    flat_tok = jnp.arange(n_pairs) // TOP_K
    order = jnp.argsort(flat_e)
    e_sorted, tok_sorted, w_sorted = flat_e[order], flat_tok[order], gates.reshape(-1)[order]
    counts = jnp.bincount(flat_e, length=N_EXPERTS)
    start = jnp.cumsum(counts) - counts
    padded = (counts + MOE_BLOCK - 1) // MOE_BLOCK * MOE_BLOCK
    pend = jnp.cumsum(padded)
    pstart = pend - padded
    dest = pstart[e_sorted] + jnp.arange(n_pairs) - start[e_sorted]
    n_blocks = (n_pairs + N_EXPERTS * (MOE_BLOCK - 1) + MOE_BLOCK - 1) // MOE_BLOCK
    xbuf = jnp.zeros((n_blocks * MOE_BLOCK, d), h.dtype).at[dest].set(h[tok_sorted])
    block_e = jnp.clip(jnp.searchsorted(pend, jnp.arange(n_blocks) * MOE_BLOCK, side='right'), 0, N_EXPERTS - 1)

    def expert_block(args):
        xb, e = args
        u = xb @ w1[e] + b1[e]
        glu = jnp.minimum(u[:, ::2], SWIGLU_LIMIT)
        lin = jnp.clip(u[:, 1::2], -SWIGLU_LIMIT, SWIGLU_LIMIT)
        return (glu * jax.nn.sigmoid(SWIGLU_ALPHA * glu) * (lin + 1)) @ w2[e] + b2[e]

    ybuf = lax.map(expert_block, (xbuf.reshape(n_blocks, MOE_BLOCK, d), block_e)).reshape(-1, d)
    y_pairs = ybuf[dest] * w_sorted[:, None].astype(h.dtype)
    return jax.ops.segment_sum(y_pairs, tok_sorted, num_segments=n_tok)

def setup_inputs(seed: int = 0) -> dict:
    key = jax.random.key(seed)
    ks = jax.random.split(key, 26)
    f32 = jnp.float32
    nrm = lambda k, shape, s: jax.random.normal(k, shape, f32) * s
    dt0 = jnp.exp(jax.random.uniform(ks[10], (DEPTH, 2, SSD_HEADS), f32, math.log(1e-3), math.log(1e-1)))
    return {
        'x': nrm(ks[0], (BATCH, SEQ, D_MODEL), 1.0),
        'c': nrm(ks[1], (BATCH, D_MODEL), 1.0),
        'ctx': nrm(ks[2], (BATCH, CTX_LEN, D_MODEL), 1.0),
        'c_ctx': nrm(ks[3], (D_MODEL,), 1.0),
        'ada_w': nrm(ks[4], (DEPTH, D_MODEL, 6 * D_MODEL), 0.5 * D_MODEL ** -0.5),
        'ada_b': nrm(ks[5], (DEPTH, 6 * D_MODEL), 0.02),
        'mix_pre_norm': 1.0 + nrm(ks[6], (DEPTH, D_MODEL), 0.02),
        'mix_post_norm': 1.0 + nrm(ks[7], (DEPTH, D_MODEL), 0.02),
        'w_in': nrm(ks[8], (DEPTH, D_MODEL, IN_COLS), D_MODEL ** -0.5),
        'w_out': nrm(ks[9], (DEPTH, D_MIX, D_MODEL), D_MIX ** -0.5),
        'ssd_conv_w': nrm(ks[11], (DEPTH, SSD_CONV, SSD_XBC), SSD_CONV ** -0.5),
        'ssd_conv_b': nrm(ks[12], (DEPTH, SSD_XBC), 0.02),
        'ssd_dt_bias': dt0 + jnp.log(-jnp.expm1(-dt0)),
        'ssd_a_log': jnp.log(jax.random.uniform(ks[13], (DEPTH, 2, SSD_HEADS), f32, 1.0, 16.0)),
        'ssd_d': 1.0 + nrm(ks[14], (DEPTH, SSD_HEADS), 0.1),
        'ssd_norm': 1.0 + nrm(ks[15], (DEPTH, SSD_INNER), 0.02),
        'hg_lb': 1.0 + nrm(ks[16], (DEPTH + 1, 2, HG_INNER), 0.1),
        'hg_norm': 1.0 + nrm(ks[17], (DEPTH, HG_INNER), 0.02),
        'ffn_pre_norm': 1.0 + nrm(ks[18], (DEPTH, D_MODEL), 0.02),
        'ffn_post_norm': 1.0 + nrm(ks[19], (DEPTH, D_MODEL), 0.02),
        'router_w': nrm(ks[20], (DEPTH, D_MODEL, N_EXPERTS), D_MODEL ** -0.5),
        'router_b': nrm(ks[21], (DEPTH, N_EXPERTS), 0.01),
        'moe_w1': nrm(ks[22], (DEPTH, N_EXPERTS, D_MODEL, 2 * D_FF), D_MODEL ** -0.5),
        'moe_b1': nrm(ks[23], (DEPTH, N_EXPERTS, 2 * D_FF), 0.02),
        'moe_w2': nrm(ks[24], (DEPTH, N_EXPERTS, D_FF, D_MODEL), D_FF ** -0.5),
        'moe_b2': nrm(ks[25], (DEPTH, N_EXPERTS, D_MODEL), 0.02),
    }

def reference(x, c, ctx, c_ctx, ada_w, ada_b, mix_pre_norm, mix_post_norm, w_in, w_out,
              ssd_conv_w, ssd_conv_b, ssd_dt_bias, ssd_a_log, ssd_d, ssd_norm, hg_lb, hg_norm,
              ffn_pre_norm, ffn_post_norm, router_w, router_b, moe_w1, moe_b1, moe_w2, moe_b2):
    bsz = x.shape[0]
    lb = jnp.cumsum(jax.nn.softmax(hg_lb.astype(jnp.float32), axis=0), axis=0)
    zero_ssd = jnp.zeros((bsz, SSD_HEADS, SSD_STATE, SSD_HEAD_DIM), jnp.float32)
    zero_hg = jnp.zeros((bsz, HG_HEADS, HG_DK, HG_DV), jnp.float32)
    for l in range(DEPTH):
        update_ctx = l < DEPTH - 1
        sh_m, sc_m, g_m, sh_f, sc_f, g_f = [m[:, None, :] for m in
                                            jnp.split(jax.nn.silu(c) @ ada_w[l] + ada_b[l], 6, axis=-1)]
        csh_m, csc_m, cg_m, csh_f, csc_f, cg_f = jnp.split(jax.nn.silu(c_ctx) @ ada_w[l] + ada_b[l], 6, axis=-1)
        ux = modulate(rmsnorm(x, mix_pre_norm[l]), sh_m, sc_m) @ w_in[l]
        uc = modulate(rmsnorm(ctx, mix_pre_norm[l]), csh_m, csc_m) @ w_in[l]
        ssd_p = (ssd_conv_w[l], ssd_conv_b[l], ssd_dt_bias[l], ssd_a_log[l], ssd_d[l], ssd_norm[l])
        yc_ssd, sf, sb = ssd_branch(uc[..., :SSD_COLS], *ssd_p, zero_ssd, zero_ssd, update_ctx)
        yx_ssd, _, _ = ssd_branch(ux[..., :SSD_COLS], *ssd_p, sf, sb, True)
        yc_hg, hf, hb = hgrn_branch(uc[..., SSD_COLS:], lb[l, 0], lb[l, 1], hg_norm[l], zero_hg, zero_hg, update_ctx)
        yx_hg, _, _ = hgrn_branch(to_col_major(ux[..., SSD_COLS:]), lb[l, 0], lb[l, 1], hg_norm[l], hf, hb, True)
        mix_x = jnp.concatenate([yx_ssd, from_col_major(yx_hg)], axis=-1) @ w_out[l]
        x = x + g_m * rmsnorm(mix_x, mix_post_norm[l])
        hx = modulate(rmsnorm(x, ffn_pre_norm[l]), sh_f, sc_f)
        moe_p = (router_w[l], router_b[l], moe_w1[l], moe_b1[l], moe_w2[l], moe_b2[l])
        if update_ctx:
            mix_c = jnp.concatenate([yc_ssd, yc_hg], axis=-1) @ w_out[l]
            ctx = ctx + cg_m * rmsnorm(mix_c, mix_post_norm[l])
            hc = modulate(rmsnorm(ctx, ffn_pre_norm[l]), csh_f, csc_f)
            n_lat = hx.shape[0] * hx.shape[1]
            f_all = moe_ffn(jnp.concatenate([hx.reshape(-1, D_MODEL), hc.reshape(-1, D_MODEL)], axis=0), *moe_p)
            fx = f_all[:n_lat].reshape(hx.shape)
            ctx = ctx + cg_f * rmsnorm(f_all[n_lat:].reshape(hc.shape), ffn_post_norm[l])
        else:
            fx = moe_ffn(hx.reshape(-1, D_MODEL), *moe_p).reshape(hx.shape)
        x = x + g_f * rmsnorm(fx, ffn_post_norm[l])
    return x


_drawn_inputs = setup_inputs


def setup_inputs(seed=0):
    import zlib

    import numpy as np

    out = dict(_drawn_inputs(seed))
    spreads = {}
    factors = {'ctx': 5.511,
     'c_ctx': 6.275,
     'mix_pre_norm': 2.938,
     'mix_post_norm': 3.113,
     'ssd_conv_b': 3.393,
     'ssd_norm': 4.904,
     'hg_lb': 8.0,
     'hg_norm': 5.884,
     'ffn_post_norm': 25.707,
     'router_b': 4.283,
     'moe_b1': 8.0,
     'moe_b2': 8.0,
     'ssd_d': 2.751}
    for name, (base, spread) in spreads.items():
        noise = np.random.default_rng([zlib.crc32(name.encode()), seed]).standard_normal(out[name].shape)
        drawn = base * np.exp(spread * noise) if base else spread * noise
        out[name] = __import__('jax').numpy.asarray(drawn.astype(out[name].dtype))
    for name, factor in factors.items():
        out[name] = (out[name] * factor).astype(out[name].dtype)
    return out
```

```python
from contextlib import ExitStack

import numpy as np
import concourse.bass as bass
from concourse import mybir

F32 = mybir.dt.float32
BF16 = mybir.dt.bfloat16
U32 = mybir.dt.uint32
ALU = mybir.AluOpType
ACT = mybir.ActivationFunctionType
AX = mybir.AxisListType.X

P = 128
D = 1024
KD = D // P
SEQ, CTX = 512, 256
GRID_W = 64
ROWS = SEQ // GRID_W
NL, NCX = SEQ // P, CTX // P
NT = NL + NCX
SH, SHD, SST, SG = 8, 64, 64, 2
SIN = SH * SHD
TAPS = 5
XBC = SIN + 2 * SG * SST
HH, HD = 4, 128
HIN = HH * HD
NE, TOPK, DFF = 32, 4, 1024
ALPHA, LIMIT = 1.702, 7.0
EPS = 1e-6
MAXB = SEQ // P
NONE = 4096.0
SSD_COLS = SIN + XBC + 2 * SH
LEVELS = [64, 32, 16, 8, 4, 2, 1]
CONV = 2 + SEQ + 4 + CTX + 2
CW = CONV - 4
CX0 = SEQ + 4

COL = dict(z=(0, SIN), xs=(SIN, SIN), bcd=(2 * SIN, XBC - SIN + 2 * SH),
           q=(SSD_COLS, HIN), ff=(SSD_COLS + HIN, HIN), fb=(SSD_COLS + 2 * HIN, HIN),
           v=(SSD_COLS + 3 * HIN, HIN), g=(SSD_COLS + 4 * HIN, HIN))
LOADS = [("ada", j) for j in range(4)] + [(n, 0) for n in ("ff", "fb", "q", "v", "xs", "bcd")] + \
        [("ada", j) for j in range(4, 12)] + [("g", 0), ("z", 0), ("out", 0), ("out", 1)]
AT = {n: i for i, n in enumerate(LOADS)}

FIRST = [("ada", j) for j in range(4)]
MAIN = [(n, t) for n in ("ff", "fb") for t in range(NT)] + [("q", h) for h in range(HH)] + [("v", t) for t in range(NT)]
BACK1 = [(n, m) for m in range(4) for n in ("xl", "xc")] + [("bl", 0), ("bc", 0), ("cl", 0), ("dt", 0)]
BACK2 = [(n, t) for n in ("g", "z") for t in range(NL)]
TAIL = [("ada", j) for j in range(4, 12)]
OUTS = [(n, t) for t in range(NL) for n in ("out0", "out1")]
UNITS = FIRST + MAIN + BACK1 + TAIL + BACK2 + OUTS
NU = {u: i for i, u in enumerate(UNITS)}


def group(u):
    n = {"xl": "xs", "xc": "xs", "bl": "bcd", "bc": "bcd", "cl": "bcd", "dt": "bcd"}.get(u[0], u[0])
    return u if n == "ada" else ("out", int(n[3])) if n.startswith("out") else (n, 0)


LAST = {group(u): NU[u] for u in UNITS}

CC, _o = {}, 0
for _n, _w in (("c", 16), ("mpre", 8), ("fpre", 8), ("cw", 30), ("cb", 6), ("adb", 48)):
    CC[_n] = slice(_o, _o + _w)
    _o += _w
NCC = _o
RR, _o = {}, 0
for _n, _w in (("lbraw", 2048), ("snorm", 512), ("hnorm", 512), ("dtb", 16), ("alog", 16), ("dsk", 8), ("rb", 32),
               ("gbias", 2048), ("post", 2048)):
    RR[_n] = _o
    _o += _w
NRR = _o
NSM = RR["gbias"] - RR["snorm"]


def consts():
    a = np.arange(P)
    le = (a[:, None] <= a[None, :])
    mats = [np.eye(P), le, le.T, a[:, None] > a[None, :], a[:, None] < a[None, :], np.ones((P, P)),
            np.broadcast_to(a[None, :], (P, P))]
    f = np.concatenate([m.astype(np.float32) for m in mats], 1)
    tok = (np.arange(NL)[None, :] * P + a[:, None]).astype(np.float32)
    f = np.concatenate([f, tok - NONE, TOPK * tok - NONE], 1)
    m = []
    for s in LEVELS[1:]:
        b, half = a // (2 * s), (a // s) % 2
        m.append((b[:, None] == b[None, :]) & (half[:, None] != half[None, :]))
    m.append(np.eye(P, dtype=bool))
    return np.ascontiguousarray(f), np.ascontiguousarray(np.concatenate([x.astype(np.uint32) for x in m], 1))


NCF = 7 * P + 2 * NL


def program(nc, x, ctx_in, cols, rows, w_ada, w_in, w_out, w_rt, w1, w2, bb, cf_in, cu_in, out):
    with ExitStack() as es:
        sems = {}

        def sem(n):
            if n not in sems:
                sems[n] = es.enter_context(nc.semaphore(n))
            return sems[n]

        def sb(n, shape, dt=F32):
            return es.enter_context(nc.sbuf_tensor(n, shape, dt))

        cf = sb("cf", [P, NCF])
        cu = sb("cu", [P, 7, P], U32)
        ident, le, ge, gt, lt, ones, iota = [cf[:, i * P:(i + 1) * P] for i in range(7)]
        tokm = cf[:, 7 * P:7 * P + NL]
        pairm = cf[:, 7 * P + NL:7 * P + 2 * NL]
        colv = sb("colv", [P, NCC])
        rowv = sb("rowv", [P, NSM])
        row = {n: rowv[:, RR[n] - RR["snorm"]:RR[n] - RR["snorm"] + w] for n, w in
               (("snorm", 512), ("hnorm", 512), ("dtb", 16), ("alog", 16), ("dsk", 8), ("rb", 32))}
        sc = sb("sc", [P, KD, 2])
        mcol = sb("mcol", [P, 16, 2])
        mf = sb("mf", [P, 16])
        arow2 = sb("arow2", [1, 512])
        Am = sb("Am", [P, KD, 2])
        Af = sb("Af", [P, KD])
        ss = sb("ss", [P, 3, 8])
        dts = sb("dts", [P, 5, NT, 16])
        ea = sb("ea", [P, 2, NL, HH])
        tot = sb("tot", [P, 3, NL, 16])
        eal = sb("eal", [P, 16])
        rt = sb("rt", [P, KD, NE])

        ARENA = 48152
        arena = sb("arena", [P, ARENA])
        pos = [0]

        def take(n):
            a = pos[0]
            pos[0] += n
            assert pos[0] <= ARENA, pos
            return a

        def at(o, n, pat=None, **kw):
            v = arena[:, o:o + n]
            return v.rearrange(pat, **kw) if pat else v

        HT, W0, LA0, K0, CXR0 = take(KD * 768), take(8192), take(4096), take(4096), take(6 * CW)
        QV0, S0, T0, LB0, HN0 = take(5120), take(4096), take(5632), take(2048), take(4096)
        hT = at(HT, KD * 768, "p (k t) -> p k t", k=KD)
        hN = at(HN0, 4096, "p (k t) -> p k t", k=KD)
        gw = at(LB0, 2048, "p (a n) -> p a n", a=2)
        W = at(W0, 8192, "p (b k n) -> p b k n", b=2, k=KD)
        la = at(LA0, 4096, "p (d c n) -> p d c n", d=2, c=NL)
        kk = at(K0, 4096, "p (d c n) -> p d c n", d=2, c=NL)
        lac = at(CXR0, 2048, "p (d c n) -> p d c n", d=2, c=NCX)
        kc = at(CXR0 + 2048, 2048, "p (d c n) -> p d c n", d=2, c=NCX)
        cv = at(CXR0, 6 * CW, "p (m n) -> p m n", m=6)
        qT = at(QV0, 2048, "p (h t) -> p h t", h=HH)
        vv = at(QV0 + 2048, 3072, "p (c n) -> p c n", c=NT)
        HS = at(S0, 4096, "p (d c n) -> p d c n", d=2, c=NL)
        Gs = at(T0, 1024, "p (d h t) -> p d h t", d=2, h=HH)
        eG = at(T0 + 1024, 1024, "p (d h t) -> p d h t", d=2, h=HH)
        kT = at(T0 + 2048, 1024, "p (d h t) -> p d h t", d=2, h=HH)
        EE = at(T0 + 3072, 2048, "p (b w h t) -> p b w h t", b=2, w=2, h=HH)
        scr = at(T0 + 5120, 512, "p (h t) -> p h t", h=HH)
        raw = at(LB0, 2 * CONV, "p (b n) -> p b n", b=2)
        lbr = at(LB0, 1024, "p (d n) -> p d n", d=2)
        oml = at(LB0 + 1024, 1024, "p (d n) -> p d n", d=2)
        xt = at(S0, 2048, "p (b n) -> p b n", b=2)
        junk = at(T0 + 3072, 1024)
        lbraw = at(T0, 2048)
        arow = at(T0 + 4096, 1024, "p (b n) -> p b n", b=2)[0:2]
        tk = at(T0, 1024, "p (b n) -> p b n", b=2)
        osb = la[:, 0]
        zz = at(LA0 + 2048, 2048, "p (c n) -> p c n", c=NL)
        gg = at(K0, 2048, "p (c n) -> p c n", c=NL)
        SS = at(K0 + 2048, 2048, "p (d c n) -> p d c n", d=2, c=NL)
        xs = at(S0, 3072, "p (t n) -> p t n", t=NT)
        Bt = at(S0 + 3072, 768, "p (t n) -> p t n", t=NT)
        vw = at(T0, 1024, "p (b n) -> p b n", b=2)
        CB = at(T0 + 1024, 512, "p (d g t) -> p d g t", d=2, g=SG)
        ES = at(T0 + 1536, 2048, "p (d h t) -> p d h t", d=2, h=SH)
        ys = at(T0 + 3584, 1024, "p (b n) -> p b n", b=2)
        junk2 = at(T0 + 4608, 1024)
        mixT = at(QV0, 4096, "p (k t) -> p k t", k=KD)
        mt = at(S0, 4096, "p (c n) -> p c n", c=NL)
        x1 = at(LA0, 4096, "p (c n) -> p c n", c=NL)
        pst = at(K0, 4096, "p (a n) -> p a n", a=4)
        x1n = at(K0, 4096, "p (c n) -> p c n", c=NL)
        hxT = at(T0, 2048, "p (b k t) -> p b k t", b=2, k=KD)
        bsrc = at(LA0, 3072)
        bparts = at(K0, 4608).bitcast(BF16).rearrange("p (r n) -> p r n", r=3)
        wr = at(0, 12 * 2048, "p (s k n) -> p s k n", s=12, k=2)
        M0 = 12 * 2048
        xg = at(M0, 1024)
        xgT = at(M0 + 1024, 1024, "p (k t) -> p k t", k=KD)
        glu, lin, sg, actv = [at(M0 + 2048 + 1024 * j, 1024, "p (f n) -> p f n", f=2) for j in range(4)]
        aT = at(M0 + 6144, 1024, "p (k t) -> p k t", k=KD)
        yv = at(M0 + 7168, 1024)
        Pm = at(M0 + 8192, 512, "p (c t) -> p c t", c=NL)
        bpt = at(M0 + 8704, 1536).bitcast(BF16)
        fin = at(0, 8192, "p (b k n) -> p b k n", b=2, k=TOPK)
        fx = at(8192, 2048, "p (b n) -> p b n", b=2)
        fo = at(8192 + 2048, 2048, "p (b n) -> p b n", b=2)
        assert M0 + 8704 + 1536 <= ARENA
        rankb = at(T0 + 2560, NL * NE * (MAXB + 1), "p (c n) -> p c n", c=NL)
        M3 = at(T0 + 3456, NL * NE, "p (c e) -> p c e", c=NL)
        OH = at(T0 + 2048, NL * TOPK * NE, "p (c k e) -> p c k e", c=NL, k=TOPK)
        lg = at(T0 + 3584, NL * NE, "p (c e) -> p c e", c=NL)
        top = sb("top", [P, NL, 8])
        topi = sb("topi", [P, NL, 8], U32)
        topf = sb("topf", [P, NL, 8])
        rhsx = at(T0 + 3200, NE * NL * 2, "p (e c w) -> p e c w", e=NE, c=NL)
        rsel = sb("rsel", [P, NL, 2])
        gate = sb("gate", [P, NL, TOPK])
        gsum = sb("gsum", [P, NL, 1])
        cm = sb("cm", [1, 4])
        cnt_u = sb("cnt_u", [1, 1], U32)
        idx = sb("idx", [P, 2], U32)
        idp = sb("idp", [P, 1], U32)
        ones3 = sb("ones3", [3, P], BF16)

        pall = es.enter_context(nc.psum_tensor("pall", [P, 8, 512], F32))
        ps = [pall[:, b, :] for b in range(8)]

        xn_d = nc.dram_tensor("xn_d", (SEQ, D), F32, kind="Internal").ap()
        x1_d = nc.dram_tensor("x1_d", (SEQ, D), F32, kind="Internal").ap()
        yp_d = nc.dram_tensor("yp_d", (SEQ * TOPK, D), F32, kind="Internal").ap()
        ada_d = nc.dram_tensor("ada_d", (8, 512), F32, kind="Internal").ap()
        bp_d = nc.dram_tensor("bp_d", (3, NE, 3 * D), BF16, kind="Internal").ap()

        def perm(ap, c=None):
            v = ap.rearrange("p (r g) -> p g r", g=GRID_W)
            n = GRID_W // NL
            return v if c is None else v[:, c * n:(c + 1) * n, :]

        def heads(ap, w=64):
            return ap.unsqueeze(2).to_broadcast([ap.shape[0], ap.shape[1], w])

        def chained(eng):
            n = {}

            def done(ins, s):
                ins.then_inc(sem(s), 1)
                n[s] = n.get(s, 0) + 1
                eng.wait_ge(sem(s), n[s])
            return done

        HSTEPS = [(d, s if d == 0 else NL - 1 - s) for s in range(NL - 1) for d in range(2)]
        STEPS = [(0, t) for t in (0, 1, 2, 3, 4)] + [(1, t) for t in (0, 1, 5, 4, 3)]
        LEVELS8 = 8
        slots1 = {}
        _b = BACK1 + TAIL
        for c in range(NL):
            for L in range(7):
                if _b:
                    slots1[c, L] = _b.pop(0)

        block = es.enter_context(nc.Block())

        @block.sync
        def _(sp):
            nc.sync.dma_start(cf[:], cf_in).then_inc(sem("consts_in"), 16)
            nc.sync.dma_start(colv[:], cols).then_inc(sem("consts_in"), 16)

            def load_x(t):
                if t >= 2:
                    sp.wait_ge(sem("x_turned"), 2 * (t - 1))
                src = ctx_in[t * P:(t + 1) * P, :] if t < NCX else x[(t - NCX) * P:(t - NCX + 1) * P, :]
                nc.sync.dma_start(xt[:, t % 2, :], src).then_inc(sem(f"x_in{t % 2}"), 16)

            def load(i):
                name, j = LOADS[i]
                if i >= 2:
                    sp.wait_ge(sem("unit_done"), LAST[LOADS[i - 2]] + 1)
                    if LOADS[i - 2] in TAIL:
                        p = LOADS[i - 2][1] - 4
                        sp.wait_ge(sem("unit_read"), NU[LOADS[i - 2]] + 1)
                        nc.sync.dma_start(ada_d[p:p + 1, :], arow2[:]).then_inc(sem("ada_out"), 16)
                if name == "ada":
                    src = w_ada[:, j * 512:(j + 1) * 512]
                elif name == "out":
                    src = w_out[:, j * 512:(j + 1) * 512]
                else:
                    src = w_in[:, COL[name][0]:COL[name][0] + COL[name][1]]
                nc.sync.dma_start(W[:, i % 2, :, 0:src.shape[1]],
                                  src.rearrange("(k p) n -> p k n", p=P)).then_inc(sem(f"w_in{i % 2}"), 16)

            load_x(0)
            load_x(1)
            load(0)
            load_x(2)
            load_x(3)
            load(1)
            load_x(4)
            load_x(5)
            o = RR["snorm"]
            nc.sync.dma_start(bsrc[0:NE, :], bb).then_inc(sem("bias_src"), 16)
            nc.sync.dma_start(lbraw, rows[:, 0:2048].to_broadcast([P, 2048])).then_inc(sem("rows_in"), 16)
            load(2)
            load(3)
            nc.sync.dma_start(cu[:], cu_in.rearrange("p (m t) -> p m t", m=7)).then_inc(sem("rows_in"), 16)
            nc.sync.dma_start(rowv[:], rows[:, o:o + NSM].to_broadcast([P, NSM])).then_inc(sem("rows_in"), 16)
            nc.sync.dma_start(rt[:], w_rt.rearrange("(k p) e -> p k e", p=P)).then_inc(sem("rows_in"), 16)
            load(4)
            load(5)
            sp.wait_ge(sem("bias_split"), 5)
            for r in range(3):
                nc.sync.dma_start(bp_d[r], bparts[0:NE, r, :]).then_inc(sem("bias_stored"), 16)
            for i in range(6, len(LOADS)):
                load(i)
            sp.wait_ge(sem("mix_read"), 2 * NL)
            sp.wait_ge(sem("ada_out"), 16 * len(TAIL))
            nc.sync.dma_start(mf[:], ada_d.rearrange("a b -> (a b)")[D:3 * D].rearrange("(m p) -> p m", p=P),
                              allow_slow_non_contiguous=True).then_inc(sem("post_in"), 16)
            for h in range(2):
                nc.sync.dma_start(gw[:, h, :], ada_d.rearrange("a (q b) -> q (a b)", q=1)[:, 3 * D * h:3 * D * h + D].to_broadcast([P, D]))\
                  .then_inc(sem("post_in"), 16)
            o = RR["gbias"]
            nc.sync.dma_start(pst, rows[:, o:o + 4096].rearrange("a (b n) -> a b n", b=4).to_broadcast([P, 4, D]))\
              .then_inc(sem("post_in"), 16)
            nc.sync.dma_start(x1, x.rearrange("(c p) n -> p c n", p=P)).then_inc(sem("res_in"), 16)
            for c in range(NL):
                sp.wait_ge(sem("x1_ready"), c + 1)
                nc.sync.dma_start(x1_d[c * P:(c + 1) * P, :], x1[:, c, :]).then_inc(sem("x1_out"), 16)
                sp.wait_ge(sem("xn_ready"), c + 1)
                nc.sync.dma_start(xn_d[c * P:(c + 1) * P, :], x1n[:, c, :]).then_inc(sem("xn_out"), 16)
            sp.wait_ge(sem("routed"), 1)
            sp.wait_ge(sem("x1_out"), 16 * NL)
            sp.wait_ge(sem("xn_out"), 16 * NL)
            sp.wait_ge(sem("bias_stored"), 48)
            blocks = sp.value_load(cnt_u[0:1, 0:1], min_val=NE, max_val=NE * MAXB)
            with sp.Fori(0, blocks) as i:
                e = i % NE
                for s in range(12):
                    if s < 8:
                        h, k = s // 4, s % 4
                        src = w1[bass.ds(e, 1), k * 256:(k + 1) * 256, h * 1024:(h + 1) * 1024]
                    else:
                        src = w2[bass.ds(e, 1), (s - 8) * 256:(s - 7) * 256, :]
                    sp.wait_ge(sem(f"slot_free{s}"), i + 1)
                    nc.sync.dma_start(wr[:, s], src.rearrange("a (k p) n -> p (a k) n", p=P)).then_inc(sem(f"slot_in{s}"), 16)
                    if s == 7:
                        sp.wait_ge(sem("bias_free"), i + 1)
                        nc.sync.dma_start(bpt[0:3, :], bp_d[:, bass.ds(e, 1), :].rearrange("r a n -> r (a n)"))\
                          .then_inc(sem("bias_in"), 16)
            sp.wait_ge(sem("all_scattered"), 1)
            for c in range(NL):
                if c >= 2:
                    sp.wait_ge(sem("fin_used"), c - 1)
                nc.sync.dma_start(fin[:, c % 2], yp_d[c * P * TOPK:(c + 1) * P * TOPK, :].rearrange("(p k) n -> p k n", k=TOPK))\
                  .then_inc(sem(f"fin_in{c % 2}"), 16)
                nc.sync.dma_start(fx[:, c % 2], x1_d[c * P:(c + 1) * P, :]).then_inc(sem(f"fin_in{c % 2}"), 16)
                if c >= 1:
                    sp.wait_ge(sem("out_ready"), c)
                    nc.sync.dma_start(out[(c - 1) * P:c * P, :], fo[:, (c - 1) % 2]).then_inc(sem(f"out_done{(c - 1) % 2}"), 16)
            sp.wait_ge(sem("out_ready"), NL)
            nc.sync.dma_start(out[(NL - 1) * P:NL * P, :], fo[:, (NL - 1) % 2]).then_inc(sem(f"out_done{(NL - 1) % 2}"), 16)
            sp.wait_ge(sem("out_done0"), 32)
            sp.wait_ge(sem("out_done1"), 32)

        @block.tensor
        def _(pe):
            mm = nc.tensor.matmul
            tp = nc.tensor.transpose

            def unit(u):
                name, j = u
                i = AT[group(u)]
                pe.wait_ge(sem(f"w_in{i % 2}"), 16 * (i // 2 + 1))
                if NU[u] >= 3:
                    pe.wait_ge(sem("unit_read"), NU[u] - 2)
                if u == ("xl", 0):
                    pe.wait_ge(sem("hn_mod"), 1)
                w, b = W[:, i % 2], ps[NU[u] % 3]
                if name == "dt":
                    for t in range(NT):
                        for k in range(KD):
                            lhs = hT[:, k, t * P:(t + 1) * P] if t < NCX else hN[:, k, (t - NCX) * P:(t - NCX + 1) * P]
                            last = mm(b[:, t * 16:(t + 1) * 16], lhs, w[:, k, 256:272],
                                      start=k == 0, stop=k == KD - 1)
                    last.then_inc(sem("unit_done"), 1)
                    return
                for k in range(KD):
                    if name == "ada":
                        o, lhs, rhs = b[0:2, :], sc[:, k, :], w[:, k, :]
                    elif name in ("ff", "fb", "v", "g"):
                        a = CTX + j * P if j < NL else (j - NL) * P
                        lhs = hT[:, k, a:a + P]
                        o, rhs = b, w[:, k, :]
                    elif name == "z":
                        o, lhs, rhs = b, hN[:, k, j * P:(j + 1) * P], w[:, k, :]
                    elif name == "q":
                        o, lhs, rhs = b, w[:, k, j * P:(j + 1) * P], hT[:, k, CTX:CTX + SEQ]
                    elif name in ("xl", "bl", "cl"):
                        a = dict(x=j * P, b=0, c=P)[name[0]]
                        o, lhs, rhs = b, w[:, k, a:a + P], hN[:, k, :]
                    elif name in ("xc", "bc"):
                        a = dict(x=j * P, b=0)[name[0]]
                        o, lhs, rhs = b[:, 0:CTX], w[:, k, a:a + P], hT[:, k, 0:CTX]
                    else:
                        o, lhs, rhs = b, mixT[:, k, j * P:(j + 1) * P], w[:, k, :]
                    last = mm(o, lhs, rhs, start=k == 0, stop=k == KD - 1)
                last.then_inc(sem("unit_done"), 1)

            def ada_turn(j):
                pe.wait_ge(sem("unit_read"), NU["ada", j] + 1)
                if j:
                    pe.wait_ge(sem("arow_read"), j)
                for m in range(4):
                    last = tp(ps[3][:, 2 * m:2 * m + 2], arow[0:2, j % 2, m * P:(m + 1) * P], ident[0:2, 0:2])
                last.then_inc(sem("arow_turned"), 1)

            pe.wait_ge(sem("consts_in"), 32)

            def turn_x(t):
                pe.wait_ge(sem("x_normed"), t + 1)
                for h in range(2):
                    n = 2 * t + h
                    if n >= 2:
                        pe.wait_ge(sem("h_read"), n - 1)
                    if n - 2 >= 2 * NCX:
                        pe.wait_ge(sem("hp_read"), n - 1 - 2 * NCX)
                    for m in range(4):
                        last = tp(ps[5 + n % 2][:, m * P:(m + 1) * P], xt[:, t % 2, (4 * h + m) * P:(4 * h + m + 1) * P], ident)
                    last.then_inc(sem("x_turned"), 1)

            turn_x(0)
            turn_x(1)
            pe.wait_ge(sem("sc_ready"), 1)
            unit(("ada", 0))
            turn_x(2)
            turn_x(3)
            unit(("ada", 1))
            ada_turn(0)
            turn_x(4)
            turn_x(5)
            unit(("ada", 2))
            ada_turn(1)
            unit(("ada", 3))
            ada_turn(2)
            ada_turn(3)
            pe.wait_ge(sem("h_mod"), 1)
            for u in MAIN:
                unit(u)

            pe.wait_ge(sem("la_ready"), 2)
            n = 0
            for d in range(2):
                for t in range(NCX):
                    if n:
                        pe.wait_ge(sem("hd_exp"), n)
                    far = 1 - t if t == d else None
                    last = mm(ps[3], (gt, lt)[d], lac[:, d, t, :], start=True, stop=far is None)
                    if far is not None:
                        last = mm(ps[3], ones, lac[:, d, far, :], start=False, stop=True)
                    last.then_inc(sem("hd_done"), 1)
                    n += 1
                pe.wait_ge(sem("hkw"), n)
                for h in range(HH):
                    sl = slice(h * HD, (h + 1) * HD)
                    for t in range(NCX):
                        last = mm(ps[4 + d][:, sl], kc[:, d, t, sl], vv[:, NL + t, sl], start=t == 0, stop=t == NCX - 1)
                last.then_inc(sem("hctx_done"), 1)
            pe.wait_ge(sem("hctx_read"), 2)
            for m, (d, c) in enumerate(HSTEPS):
                pe.wait_ge(sem("hd_exp"), n)
                mm(ps[3], (gt, lt)[d], la[:, d, c, :], start=True, stop=True).then_inc(sem("hd_done"), 1)
                n += 1
                if m:
                    pe.wait_ge(sem("hea"), m)
                for h in range(HH):
                    last = mm(ps[5][:, h:h + 1], la[:, d, c, h * HD:(h + 1) * HD], ones[:, 0:1], start=True, stop=True)
                last.then_inc(sem("hea_done"), 1)
                pe.wait_ge(sem("hkw"), n)
                if m:
                    pe.wait_ge(sem("hu_read"), m)
                for h in range(HH):
                    sl = slice(h * HD, (h + 1) * HD)
                    last = mm(ps[4][:, sl], tk[:, m % 2, sl], vv[:, c, sl], start=True, stop=True)
                last.then_inc(sem("hu_done"), 1)
            pe.wait_ge(sem("hu_read"), len(HSTEPS))
            pe.wait_ge(sem("hea"), len(HSTEPS))
            lv = 0
            for c in range(NL):
                if c:
                    pe.wait_ge(sem("g_read"), 2 * c)
                for d in range(2):
                    for h in range(HH):
                        sl = slice(h * HD, (h + 1) * HD)
                        last = mm(ps[3 + d][:, sl], la[:, d, c, sl], (le, ge)[d], start=True, stop=True)
                    last.then_inc(sem("g_done"), 1)
                if c:
                    pe.wait_ge(sem("level_read"), 8 * c)
                for d in range(2):
                    for h in range(HH):
                        last = tp(ps[5 + d][:, h * P:(h + 1) * P], kk[:, d, c, h * HD:(h + 1) * HD], ident)
                    last.then_inc(sem("kt_done"), 1)
                pe.wait_ge(sem("kt_read"), 2 * (c + 1))
                for L in range(8):
                    pe.wait_ge(sem("level_ready"), lv + 1)
                    if lv >= 2:
                        pe.wait_ge(sem("level_read"), lv - 1)
                    for h in range(HH):
                        rhs = EE[:, lv % 2, 0, h, :] if L < 7 else qT[:, h, c * P:(c + 1) * P]
                        last = mm(ps[5 + lv % 2][:, h * P:(h + 1) * P], EE[:, lv % 2, 1, h, :], rhs, start=True, stop=True)
                    last.then_inc(sem("level_done"), 1)
                    lv += 1
                    if (c, L) in slots1:
                        unit(slots1[c, L])
                pe.wait_ge(sem("level_read"), lv)
                if c:
                    pe.wait_ge(sem("ho_read"), c)
                for h in range(HH):
                    sl = slice(h * HD, (h + 1) * HD)
                    mm(ps[7][:, sl], scr[:, h, :], vv[:, c, sl], start=True, stop=False)
                    mm(ps[7][:, sl], eG[:, 0, h, :], HS[:, 0, c, sl], start=False, stop=False)
                    last = mm(ps[7][:, sl], eG[:, 1, h, :], HS[:, 1, c, sl], start=False, stop=True)
                last.then_inc(sem("ho_done"), 1)

            pe.wait_ge(sem("cv_ready"), 1)
            pe.wait_ge(sem("ho_read"), NL)
            for t in range(NT):
                o = CX0 + t * P if t < NCX else (t - NCX) * P
                if t:
                    pe.wait_ge(sem("xs_read"), t)
                for m in range(5):
                    b = ps[3][:, m * P:(m + 1) * P] if m < 4 else ps[4][:, 0:P]
                    last = tp(b, cv[:, m, o:o + P], ident)
                last.then_inc(sem("xs_turned"), 1)
            pe.wait_ge(sem("dt_ready"), 2)
            LG = dts[:, 1]
            for t in range(NT):
                for d in range(2):
                    sl = slice(8 * d, 8 * d + 8)
                    o = ps[5][:, t * 16 + 8 * d:t * 16 + 8 * d + 8]
                    far = 1 - t if t < NCX and t == d else None
                    last = mm(o, (gt, lt)[d], LG[:, t, sl], start=True, stop=far is None)
                    if far is not None:
                        last = mm(o, ones, LG[:, far, sl], start=False, stop=True)
            for c in range(NL):
                mm(ps[5][:, 128 + 16 * c:144 + 16 * c], ones, LG[:, NCX + c, :], start=True, stop=True)
                for d in range(2):
                    a = 256 + 16 * c + 8 * d
                    last = mm(ps[5][:, a:a + 8], (le, ge)[d], LG[:, NCX + c, 8 * d:8 * d + 8], start=True, stop=True)
            last.then_inc(sem("sdec_done"), 1)
            back = list(BACK2)
            pe.wait_ge(sem("xs_read"), NT)
            done = 0
            for n, (d, t) in enumerate(STEPS):
                if t == 0:
                    continue
                pe.wait_ge(sem("svw"), n + 1)
                if done:
                    pe.wait_ge(sem("su_read"), done)
                for g in range(SG):
                    o = ps[6][64 * g:64 * g + 64, 0:256]
                    sl, sv = slice(64 * g, 64 * g + 64), slice(256 * g, 256 * g + 256)
                    if t == 1:
                        mm(o, Bt[:, 0, sl], vw[:, (n - 1) % 2, sv], start=True, stop=False)
                        last = mm(o, Bt[:, 1, sl], vw[:, n % 2, sv], start=False, stop=True)
                    else:
                        last = mm(o, Bt[:, t, sl], vw[:, n % 2, sv], start=True, stop=True)
                last.then_inc(sem("su_done"), 1)
                done += 1
                if t > 1:
                    unit(back.pop(0))
            pe.wait_ge(sem("su_read"), done)
            BT, CT = cv[:, 4], cv[:, 5]
            for c in range(NL):
                sl = slice(c * P, (c + 1) * P)
                if c:
                    pe.wait_ge(sem("sy_read"), c)
                for g in range(SG):
                    gs = slice(64 * g, 64 * g + 64)
                    last = mm(ps[3 + 3 * g][:, 0:P], BT[gs, sl], CT[gs, sl], start=True, stop=True)
                last.then_inc(sem("cb_done"), 1)
                for q4 in range(4):
                    d, hf = q4 // 2, q4 % 2
                    m = 4 * c + q4
                    if m >= 2:
                        pe.wait_ge(sem("se_read"), m - 1)
                    for h in range(4):
                        a = 8 * d + 4 * hf + h
                        last = mm(ps[4 + m % 2][:, h * P:(h + 1) * P], LG[:, NCX + c, a:a + 1].to_broadcast([P, P]), (le, ge)[d],
                                  start=True, stop=True)
                    last.then_inc(sem("se_done"), 1)
                if back and c < 2:
                    unit(back.pop(0))
                pe.wait_ge(sem("sst"), 4 * c + 4)
                for h in range(SH):
                    for d in range(2):
                        last = mm(ps[6][:, h * 64:(h + 1) * 64], ES[:, d, h, :], vw[:, d, h * 64:(h + 1) * 64],
                                  start=d == 0, stop=d == 1)
                for g in range(SG):
                    gs = slice(64 * g, 64 * g + 64)
                    for d in range(2):
                        last = mm(ps[7 if g == 0 else 3][:, 256 * d:256 * d + 256], CT[gs, sl], SS[gs, d, c, :], start=True, stop=True)
                last.then_inc(sem("sy_done"), 1)
                pe.wait_ge(sem("mix_ready"), c + 1)
                for m in range(4):
                    last = tp(ps[4][:, m * P:(m + 1) * P], ys[:, 0, m * P:(m + 1) * P], ident)
                last.then_inc(sem("mix_turned"), 1)
                pe.wait_ge(sem("mix_read"), c + 1)
            for c in range(NL):
                pe.wait_ge(sem("mix_ready"), NL + c + 1)
                if c >= 2:
                    pe.wait_ge(sem("mix_read"), NL + c - 1)
                for m in range(4):
                    last = tp(ps[4 + c % 2][:, m * P:(m + 1) * P], osb[:, c, m * P:(m + 1) * P], ident)
                last.then_inc(sem("mix_turned"), 1)
            pe.wait_ge(sem("mix_read"), 2 * NL)
            outs = list(OUTS)
            for _ in range(4):
                unit(outs.pop(0))
            for c in range(NL):
                for _ in range(min(2, len(outs))):
                    unit(outs.pop(0))
                pe.wait_ge(sem("xn_ready"), c + 1)
                for h in range(2):
                    n = 2 * c + h
                    if n >= 2:
                        pe.wait_ge(sem("hx_read"), n - 1)
                    for m in range(4):
                        last = tp(ps[5 + n % 2][:, m * P:(m + 1) * P], x1n[:, c, (4 * h + m) * P:(4 * h + m + 1) * P], ident)
                    last.then_inc(sem("hx_turned"), 1)
                pe.wait_ge(sem("hx_read"), 2 * (c + 1))
                for k in range(KD):
                    last = mm(ps[3][:, c * NE:(c + 1) * NE], hxT[:, c % 2, k, :], rt[:, k, :], start=k == 0, stop=k == KD - 1)
                last.then_inc(sem("logit_done"), 1)
            pe.wait_ge(sem("chosen"), 1)
            for c in range(NL):
                for b in range(c + 1):
                    mm(ps[4][:, c * NE:(c + 1) * NE], lt if b == c else ones, M3[:, b, :], start=b == 0, stop=b == c)
            for b in range(NL):
                last = mm(ps[4][:, P:P + NE], ones, M3[:, b, :], start=b == 0, stop=b == NL - 1)
            last.then_inc(sem("rank_done"), 1)

            pe.wait_ge(sem("routed"), 1)
            blocks = pe.value_load(cnt_u[0:1, 0:1], min_val=NE, max_val=NE * MAXB)
            for s in range(12):
                pe.sem_inc(sem(f"slot_free{s}"), 1)
            pe.sem_inc(sem("bias_free"), 1)

            def find_slots():
                for c in range(NL):
                    last = mm(ps[7][:, 0:2], Pm[:, c, :], rsel[:, c, :], start=c == 0, stop=c == NL - 1)
                last.then_inc(sem("slots_done"), 1)

            def turn_rows(h):
                for m in range(4):
                    last = tp(ps[6 + h][:, m * P:(m + 1) * P], xg[:, (4 * h + m) * P:(4 * h + m + 1) * P], ident)
                last.then_inc(sem("xg_turned"), 1)

            pe.wait_ge(sem("pm_ready"), 1)
            find_slots()
            pe.wait_ge(sem("xg_in"), 16)
            turn_rows(0)
            turn_rows(1)
            with pe.Fori(0, blocks) as i:
                pe.wait_ge(sem("xgT_ready"), 2 * i + 2)
                pe.wait_ge(sem("bias_in"), 16 * i + 16)
                for hf in range(2):
                    pe.wait_ge(sem("u_read"), 2 * i + hf + 1)
                    for n2 in range(2):
                        o = hf * 1024 + n2 * 512
                        mm(ps[2 * hf + n2], ones3[:], bpt[0:3, o:o + 512], start=True, stop=False)
                    for s in range(4):
                        pe.wait_ge(sem(f"slot_in{4 * hf + s}"), 16 * i + 16)
                        for k2 in range(2):
                            for n2 in range(2):
                                k = 2 * s + k2
                                last = mm(ps[2 * hf + n2], xgT[:, k, :], wr[:, 4 * hf + s, k2, n2 * 512:(n2 + 1) * 512],
                                          start=False, stop=k == KD - 1)
                        last.then_inc(sem(f"slot_free{4 * hf + s}"), 1)
                        if hf == 1 and s == 2:
                            pe.wait_ge(sem("act_ready"), 2 * i + 1)
                            for m in range(4):
                                last = tp(ps[6][:, m * P:(m + 1) * P], actv[:, 0, m * P:(m + 1) * P], ident)
                            last.then_inc(sem("act_turned"), 1)
                    if hf == 0:
                        pe.wait_ge(sem("pm_ready"), i + 2)
                        find_slots()
                pe.wait_ge(sem("y_ready"), i + 1)
                for n2 in range(2):
                    last = mm(ps[4 + n2], ones3[:], bpt[0:3, 2048 + n2 * 512:2560 + n2 * 512], start=True, stop=False)
                last.then_inc(sem("bias_free"), 1)
                for hf in range(2):
                    if hf == 1:
                        pe.wait_ge(sem("act_ready"), 2 * i + 2)
                        pe.wait_ge(sem("idx_ready"), i + 2)
                        for m in range(4):
                            last = tp(ps[7][:, m * P:(m + 1) * P], actv[:, 1, m * P:(m + 1) * P], ident)
                        last.then_inc(sem("act_turned"), 1)
                        pe.wait_ge(sem("xg_in"), 16 * i + 32)
                        turn_rows(0)
                    pe.wait_ge(sem("aT_ready"), 2 * i + hf + 1)
                    if hf == 1:
                        turn_rows(1)
                    for s in range(2 * hf, 2 * hf + 2):
                        pe.wait_ge(sem(f"slot_in{8 + s}"), 16 * i + 16)
                        for k2 in range(2):
                            for n2 in range(2):
                                k = 2 * s + k2
                                last = mm(ps[4 + n2], aT[:, k, :], wr[:, 8 + s, k2, n2 * 512:(n2 + 1) * 512],
                                          start=False, stop=k == KD - 1)
                        last.then_inc(sem(f"slot_free{8 + s}"), 1)

        @block.scalar
        def _(act):
            A = nc.scalar.activation
            done = chained(act)

            def root(n, width, base):
                pass

            act.wait_ge(sem("consts_in"), 32)
            A(sc[:].rearrange("p k s -> p (k s)"), colv[:, CC["c"]], ACT.Silu).then_inc(sem("sc_ready"), 1)

            def read(u):
                name, j = u
                act.wait_ge(sem("unit_done"), NU[u] + 1)
                b = ps[NU[u] % 3]
                if name == "ada":
                    if j >= 4:
                        if j > 4:
                            act.wait_ge(sem("ada_out"), 16 * (j - 4))
                        i = A(arow2[:], b[0:1, :], ACT.Copy)
                    else:
                        if j >= 2:
                            act.wait_ge(sem("arow_turned"), j - 1)
                        i = A(arow[:, j % 2, :], b[0:2, :], ACT.Copy)
                elif name in ("ff", "fb"):
                    d = int(name == "fb")
                    i = A(kk[:, d, j, :] if j < NL else kc[:, d, j - NL, :], b, ACT.Sigmoid)
                elif name == "q":
                    i = A(qT[:, j, :], b, ACT.Silu)
                elif name == "v":
                    i = A(vv[:, j, :], b, ACT.Copy)
                elif name in ("xl", "bl", "cl", "xc", "bc"):
                    m = dict(x=j, b=4, c=5)[name[0]]
                    if m >= 2:
                        act.wait_ge(sem("conv_done"), m - 1)
                    else:
                        act.wait_ge(sem("raw_zeroed"), 1)
                    i = A(raw[:, m % 2, 2:2 + SEQ], b, ACT.Copy) if name[1] == "l" else \
                        A(raw[:, m % 2, 6 + SEQ:6 + SEQ + CTX], b[:, 0:CTX], ACT.Copy)
                elif name == "dt":
                    i = A(dts[:, 0].rearrange("p t n -> p (t n)"), b[:, 0:NT * 16], ACT.Copy)
                elif name == "g":
                    i = A(gg[:, j, :], b, ACT.Silu)
                elif name == "z":
                    i = A(zz[:, j, :], b, ACT.Silu)
                else:
                    i = A(mt[:, j, (name == "out1") * 512:(name == "out1") * 512 + 512], b, ACT.Copy)
                i.then_inc(sem("unit_read"), 1)

            def square_x(t):
                act.wait_ge(sem(f"x_in{t % 2}"), 16 * (t // 2 + 1))
                done(A(junk, xt[:, t % 2, :], ACT.Square, accum_out=ss[:, 0, t:t + 1]), "x_sq")
                act.wait_ge(sem("x_ms"), t + 1)
                A(ss[:, 2, t:t + 1], ss[:, 1, t:t + 1], ACT.Sqrt).then_inc(sem("x_rt"), 1)

            def order_x(t):
                for h in range(2):
                    n, c = 2 * t + h, t - NCX
                    act.wait_ge(sem("h_read"), n + 1)
                    to = hT[:, 4 * h:4 * h + 4, CTX:CTX + SEQ].rearrange("p k (g r) -> p k r g", r=ROWS)
                    src = ps[5 + n % 2].rearrange("p (k r g) -> p k r g", k=4, r=2)
                    for r in range(2):
                        last = A(to[:, :, 2 * c + r, :], src[:, :, r, :], ACT.Copy)
                    last.then_inc(sem("hp_read"), 1)

            square_x(0)
            square_x(1)
            for t in range(NCX, NT):
                square_x(t)
                if t > NCX:
                    order_x(t - 1)
                if t == 3:
                    read(("ada", 0))
                if t == 5:
                    read(("ada", 1))
            order_x(NT - 1)
            read(("ada", 2))
            read(("ada", 3))
            act.wait_ge(sem("lb_diff"), 1)
            A(lbr.rearrange("p d n -> p (d n)"), lbraw[:, 0:1024], ACT.Sigmoid).then_inc(sem("lb_sig"), 1)
            act.wait_ge(sem("am_ready"), 1)
            act.wait_ge(sem("h_read"), 2 * NT)
            for k in range(KD):
                last = A(hN[:, k, :], hN[:, k, :], ACT.Identity, bias=mcol[:, k, 0:1], scale=Am[:, k, 0:1])
            last.then_inc(sem("hn_mod"), 1)
            act.wait_ge(sem("bias_stored"), 48)
            for u in MAIN:
                read(u)
            act.wait_ge(sem("f_ready"), 2 * NT)
            A(at(LA0, 4096), at(LA0, 4096), ACT.Ln).then_inc(sem("la_ready"), 1)
            A(at(CXR0, 2048), at(CXR0, 2048), ACT.Ln).then_inc(sem("la_ready"), 1)
            n = 0
            for _ in range(2 * NCX):
                if n >= 2:
                    act.wait_ge(sem("hkw"), n - 1)
                act.wait_ge(sem("hd_done"), n + 1)
                A(tk[:, n % 2, :], ps[3], ACT.Exp).then_inc(sem("hd_exp"), 1)
                n += 1
            for m, (d, c) in enumerate(HSTEPS):
                act.wait_ge(sem("hkw"), min(n - 1, 2 * NCX))
                if m >= 2:
                    act.wait_ge(sem("hu_done"), m - 1)
                act.wait_ge(sem("hd_done"), n + 1)
                A(tk[:, n % 2, :], ps[3], ACT.Exp).then_inc(sem("hd_exp"), 1)
                n += 1
                act.wait_ge(sem("hea_done"), m + 1)
                A(ea[:, d, c, :], ps[5][:, 0:HH], ACT.Exp).then_inc(sem("hea"), 1)
            lv = 0
            for c in range(NL):
                if c:
                    act.wait_ge(sem("ho_done"), c)
                for d in range(2):
                    act.wait_ge(sem("g_done"), 2 * c + d + 1)
                    A(Gs[:, d].rearrange("p h t -> p (h t)"), ps[3 + d], ACT.Copy)
                    A(eG[:, d].rearrange("p h t -> p (h t)"), ps[3 + d], ACT.Exp).then_inc(sem("g_read"), 1)

                def level(L, lv):
                    act.wait_ge(sem("e_sub"), 7 * c + L + 1)
                    e = EE[:, lv % 2].rearrange("p w h t -> p (w h t)")
                    A(e, e, ACT.Exp).then_inc(sem("e_exp"), 1)

                level(0, lv)
                for L in range(8):
                    if L + 1 < 7:
                        level(L + 1, lv + 1)
                    if (c, L) in slots1:
                        read(slots1[c, L])
                    lv += 1
                act.wait_ge(sem("ho_done"), c + 1)
                A(osb[:, c, :], ps[7], ACT.Copy).then_inc(sem("ho_read"), 1)
            act.wait_ge(sem("conv_done"), 6)
            A(at(CXR0, 6 * CW), at(CXR0, 6 * CW), ACT.Silu).then_inc(sem("cv_ready"), 1)
            act.wait_ge(sem("dt_abs"), 1)
            t3 = dts[:, 3].rearrange("p t n -> p (t n)")
            done(A(t3, t3, ACT.Exp, scale=-1.0), "a_chain")
            done(A(t3, t3, ACT.Ln, bias=1.0), "a_chain")
            A(eal[:], row["alog"], ACT.Exp).then_inc(sem("dt_log"), 1)
            act.wait_ge(sem("sdec_done"), 1)
            A(t3, ps[5][:, 0:NT * 16], ACT.Exp)
            A(tot[:, 0].rearrange("p c n -> p (c n)"), ps[5][:, 128:192], ACT.Exp)
            A(tot[:, 1].rearrange("p c n -> p (c n)"), ps[5][:, 256:320], ACT.Copy)
            A(tot[:, 2].rearrange("p c n -> p (c n)"), ps[5][:, 256:320], ACT.Exp).then_inc(sem("sdec_exp"), 1)
            back = list(BACK2)
            for d, t in STEPS:
                if t > 1:
                    read(back.pop(0))
            for c in range(NL):
                for q4 in range(4):
                    d, hf = q4 // 2, q4 % 2
                    act.wait_ge(sem("se_read"), 4 * c + q4 + 1)
                    e = ES[:, d, 4 * hf:4 * hf + 4, :].rearrange("p h t -> p (h t)")
                    A(e, e, ACT.Exp).then_inc(sem("se_exp"), 1)
                if back and c < 2:
                    read(back.pop(0))
                act.wait_ge(sem("y_gated"), c + 1)
                done(A(junk2[:, 0:SIN], ys[:, 0, :], ACT.Square, accum_out=ss[:, 0, c:c + 1]), "y_sq")
                act.wait_ge(sem("y_ms"), c + 1)
                A(ss[:, 2, c:c + 1], ss[:, 1, c:c + 1], ACT.Sqrt).then_inc(sem("y_rt"), 1)
            for c in range(NL):
                if c:
                    act.wait_ge(sem("mix_ready"), NL + c)
                for h in range(HH):
                    sl = slice(h * HD, (h + 1) * HD)
                    done(A(junk2[:, sl], osb[:, c, sl], ACT.Square, accum_out=ss[:, 0, h:h + 1]), "o_sq")
                act.wait_ge(sem("o_ms"), c + 1)
                A(ss[:, 2, 0:HH], ss[:, 1, 0:HH], ACT.Sqrt).then_inc(sem("o_rt"), 1)
            outs = list(OUTS)
            read(outs.pop(0))
            read(outs.pop(0))
            for c in range(NL):
                for s, src in (("m", mt), ("n", x1)):
                    if s == "m":
                        act.wait_ge(sem("unit_read"), NU["out1", c] + 1)
                    if s == "n":
                        act.wait_ge(sem("x1_ready"), c + 1)
                    done(A(junk2, src[:, c, :], ACT.Square, accum_out=ss[:, 0, c:c + 1]), f"{s}_sq")
                    act.wait_ge(sem(f"{s}_ms"), c + 1)
                    A(ss[:, 2, c:c + 1], ss[:, 1, c:c + 1], ACT.Sqrt).then_inc(sem(f"{s}_rt"), 1)
                    if s == "m" and outs:
                        read(outs.pop(0))
                        read(outs.pop(0))
            act.wait_ge(sem("top_sub"), 1)
            A(gate[:].rearrange("p c k -> p (c k)"), gate[:].rearrange("p c k -> p (c k)"), ACT.Exp).then_inc(sem("top_exp"), 1)
            act.wait_ge(sem("routed"), 1)
            blocks = act.value_load(cnt_u[0:1, 0:1], min_val=NE, max_val=NE * MAXB)
            act.sem_inc(sem("y_ready"), 1)

            def spread(h):
                for m in range(4):
                    k = 4 * h + m
                    last = A(xgT[:, k, :], ps[6 + h][:, m * P:(m + 1) * P], ACT.Identity, bias=mf[:, k:k + 1], scale=Af[:, k:k + 1])
                last.then_inc(sem("xgT_ready"), 1)

            for h in range(2):
                act.wait_ge(sem("xg_turned"), h + 1)
                spread(h)
            with act.Fori(0, blocks) as i:
                for hf in range(2):
                    act.wait_ge(sem("glu_ready"), 2 * i + hf + 1)
                    A(sg[:, hf, :], glu[:, hf, :], ACT.Sigmoid, scale=ALPHA).then_inc(sem("sg_ready"), 1)
                    act.wait_ge(sem("act_turned"), 2 * i + hf + 1)
                    A(aT[:, 4 * hf:4 * hf + 4, :].rearrange("p k t -> p (k t)"), ps[6 + hf], ACT.Copy).then_inc(sem("aT_ready"), 1)
                for h in range(2):
                    act.wait_ge(sem("xg_turned"), 2 * i + h + 3)
                    spread(h)
                act.wait_ge(sem("slot_free11"), i + 2)
                act.wait_ge(sem("block_moved"), i + 1)
                A(yv, pall[:, 4:6, :].rearrange("p b n -> p (b n)"), ACT.Copy).then_inc(sem("y_ready"), 1)
            for c in range(NL):
                act.wait_ge(sem("f_sum"), c + 1)
                done(A(junk2, fo[:, c % 2], ACT.Square, accum_out=ss[:, 0, c:c + 1]), "f_sq")
                act.wait_ge(sem("f_ms"), c + 1)
                A(ss[:, 2, c:c + 1], ss[:, 1, c:c + 1], ACT.Sqrt).then_inc(sem("f_rt"), 1)

        @block.vector
        def _(v):
            tt, ts, stt, cp = nc.vector.tensor_tensor, nc.vector.tensor_scalar, nc.vector.scalar_tensor_tensor, nc.vector.tensor_copy
            done = chained(v)

            def mean(s, col, width, count):
                v.wait_ge(sem(f"{s}_sq"), count * (col.stop - col.start if s == "o" else 1))
                done(ts(ss[:, 1, col], ss[:, 0, col], 1.0 / width, EPS, ALU.mult, ALU.add), f"{s}_ms")
                v.wait_ge(sem(f"{s}_rt"), count)
                done(nc.vector.reciprocal(ss[:, 1, col], ss[:, 2, col]), "v_chain")

            v.memset(ones3[:], 1.0)
            def modulation(j):
                v.wait_ge(sem("arow_turned"), j + 1)
                s = slice(4 * j, 4 * j + 4)
                adb = colv[:, CC["adb"]][:, s]
                done(tt(mcol[:, s, :], ps[3][:, 0:8].rearrange("p (m s) -> p m s", s=2), heads(adb, 2), ALU.add), "arow_read")

            def norm_x(t):
                mean("x", slice(t, t + 1), D, t + 1)
                done(ts(xt[:, t % 2, :], xt[:, t % 2, :], ss[:, 1, t:t + 1], None, ALU.mult), "x_normed")

            def store_x(t):
                for h in range(2):
                    v.wait_ge(sem("x_turned"), 2 * t + h + 1)
                    ks = slice(4 * h, 4 * h + 4)
                    to = hT[:, ks, t * P:(t + 1) * P] if t < NCX else hN[:, ks, (t - NCX) * P:(t - NCX + 1) * P]
                    done(cp(to, ps[5 + (2 * t + h) % 2].rearrange("p (k t) -> p k t", k=4)), "h_read")

            for t in range(NT + 1):
                if t < NT:
                    norm_x(t)
                if t:
                    store_x(t - 1)
            v.wait_ge(sem("bias_src"), 16)
            b = bsrc[0:NE, :]
            for r in range(3):
                done(cp(bparts[0:NE, r, :], b), "bias_split")
                if r < 2:
                    done(tt(b, b, bparts[0:NE, r, :], ALU.subtract), "bias_split")
            v.wait_ge(sem("rows_in"), 64)
            done(tt(lbraw[:, 0:1024], lbraw[:, 0:1024], lbraw[:, 1024:2048], ALU.subtract), "lb_diff")

            for j in range(4):
                modulation(j)
            v.wait_ge(sem("consts_in"), 32)
            done(stt(Am[:], mcol[:, 8:16, :], 1.0, heads(colv[:, CC["mpre"]], 2), ALU.add, ALU.mult), "am_ready")
            v.wait_ge(sem("hp_read"), 2 * NL)
            for k in range(KD):
                for s, o in ((1, hT[:, k, 0:CTX]), (0, hT[:, k, CTX:CTX + SEQ])):
                    last = ts(o, o, Am[:, k, s:s + 1], mcol[:, k, s:s + 1], ALU.mult, ALU.add)
            last.then_inc(sem("h_mod"), 1)
            v.wait_ge(sem("lb_sig"), 1)
            done(ts(oml, lbr, -1.0, 1.0, ALU.mult, ALU.add), "v_chain")
            for u in MAIN:
                if u[0] in ("ff", "fb"):
                    d, j = int(u[0] == "fb"), u[1]
                    v.wait_ge(sem("unit_read"), NU[u] + 1)
                    if j == 0:
                        v.wait_ge(sem("bias_stored"), 48)
                    kd, ld = (kk[:, d, j], la[:, d, j]) if j < NL else (kc[:, d, j - NL], lac[:, d, j - NL])
                    done(tt(ld, kd, oml[:, d], ALU.mult), "v_chain")
                    done(tt(ld, ld, lbr[:, d], ALU.add), "v_chain")
                    done(ts(kd, ld, -1.0, 1.0, ALU.mult, ALU.add), "f_ready")
                elif u[0] == "q":
                    v.wait_ge(sem("unit_read"), NU[u] + 1)
                    done(ts(qT[:, u[1]], qT[:, u[1]], HD ** -0.5, None, ALU.mult), "v_chain")
            done(v.memset(raw, 0.0), "raw_zeroed")
            n = 0
            for d in range(2):
                for t in range(NCX):
                    v.wait_ge(sem("hd_exp"), n + 1)
                    done(tt(kc[:, d, t], kc[:, d, t], tk[:, n % 2], ALU.mult), "hkw")
                    n += 1
                v.wait_ge(sem("hctx_done"), d + 1)
                done(cp(HS[:, d, d * (NL - 1)], ps[4 + d]), "hctx_read")
            for m, (d, c) in enumerate(HSTEPS):
                v.wait_ge(sem("hd_exp"), n + 1)
                done(tt(tk[:, n % 2], tk[:, n % 2], kk[:, d, c], ALU.mult), "hkw")
                n += 1
                v.wait_ge(sem("hea"), m + 1)
                v.wait_ge(sem("hu_done"), m + 1)
                for h in range(HH):
                    sl = slice(h * HD, (h + 1) * HD)
                    last = stt(HS[:, d, c + 1 - 2 * d, sl], HS[:, d, c, sl], ea[:, d, c, h:h + 1], ps[4][:, sl], ALU.mult, ALU.add)
                done(last, "hu_read")
            lv = 0
            ready = {("xc", m): m for m in range(4)}
            ready.update({("bc", 0): 4, ("cl", 0): 5})

            def conv(m):
                cw, cb = colv[:, CC["cw"]], colv[:, CC["cb"]]
                r = raw[:, m % 2]
                done(ts(cv[:, m, :], r[:, 0:CW], cw[:, 5 * m:5 * m + 1], cb[:, m:m + 1], ALU.mult, ALU.add), "v_chain")
                for k in range(1, TAPS):
                    done(stt(cv[:, m, :], r[:, k:k + CW], cw[:, 5 * m + k:5 * m + k + 1], cv[:, m, :], ALU.mult, ALU.add),
                         "conv_done" if k == TAPS - 1 else "v_chain")

            for c in range(NL):
                cs = slice(c * P, (c + 1) * P)
                for d in range(2):
                    v.wait_ge(sem("kt_done"), 2 * c + d + 1)
                    done(cp(kT[:, d].rearrange("p h t -> p (h t)"), ps[5 + d]), "kt_read")
                for d in range(2):
                    v.wait_ge(sem("g_read"), 2 * c + d + 1)
                    done(tt(eG[:, d], eG[:, d], qT[:, :, cs], ALU.mult), "v_chain")

                def halves(t, s):
                    w = t.rearrange("p h (b w s) -> p (h b) w s", w=2, s=s)
                    return w[:, :, 0, :], w[:, :, 1, :]

                def subtract(L, lv):
                    s = LEVELS[L]
                    if lv >= 2:
                        v.wait_ge(sem("level_done"), lv - 1)
                    gfl, gfr = halves(Gs[:, 0], s)
                    gbl, gbr = halves(Gs[:, 1], s)
                    ql, qr = halves(EE[:, lv % 2, 0], s)
                    kl, kr = halves(EE[:, lv % 2, 1], s)
                    sh = list(gfl.shape)
                    mf, mb = gfl[:, :, s - 1:s].to_broadcast(sh), gbr[:, :, 0:1].to_broadcast(sh)
                    tt(qr, gfr, mf, ALU.subtract)
                    tt(ql, gbl, mb, ALU.subtract)
                    tt(kl, mf, gfl, ALU.subtract)
                    tt(kr, mb, gbr, ALU.subtract).then_inc(sem("e_sub"), 1)

                def multiply(L, lv):
                    s = LEVELS[L]
                    v.wait_ge(sem("e_exp"), 7 * c + L + 1)
                    kl, kr = halves(EE[:, lv % 2, 1], s)
                    fl, _ = halves(kT[:, 0], s)
                    _, br = halves(kT[:, 1], s)
                    tt(EE[:, lv % 2, 0], EE[:, lv % 2, 0], qT[:, :, cs], ALU.mult)
                    tt(kl, kl, fl, ALU.mult)
                    tt(kr, kr, br, ALU.mult).then_inc(sem("level_ready"), 1)

                def keep(L, lv):
                    v.wait_ge(sem("level_done"), lv + 1)
                    src = ps[5 + lv % 2].rearrange("p (h t) -> p h t", h=HH)
                    if L == 0:
                        ins = cp(scr, src)
                    else:
                        ins = nc.vector.copy_predicated(scr, cu[:, L - 1, :].unsqueeze(1).to_broadcast([P, HH, P]), src)
                    done(ins, "level_read")

                if c:
                    v.wait_ge(sem("ho_done"), c)
                subtract(0, lv)
                for L in range(8):
                    if L + 1 < 7:
                        subtract(L + 1, lv + 1)
                    if L < 7:
                        multiply(L, lv)
                    else:
                        v.wait_ge(sem("level_done"), lv - 1)
                        tt(EE[:, lv % 2, 1], kT[:, 0], kT[:, 1], ALU.add).then_inc(sem("level_ready"), 1)
                    if L:
                        keep(L - 1, lv - 1)
                    if (c, L - 1) in slots1 and slots1[c, L - 1] in ready:
                        v.wait_ge(sem("unit_read"), NU[slots1[c, L - 1]] + 1)
                        conv(ready[slots1[c, L - 1]])
                    lv += 1
                keep(7, lv - 1)

            v.wait_ge(sem("unit_read"), NU["dt", 0] + 1)
            r0, lg_, dt_, t3, wt = [dts[:, j] for j in range(5)]
            done(tt(r0, r0, row["dtb"].unsqueeze(1).to_broadcast([P, NT, 16]), ALU.add), "v_chain")
            done(stt(t3, r0, -1.0, r0, ALU.mult, ALU.max), "dt_abs")
            done(ts(dt_, r0, 0.0, None, ALU.max), "v_chain")
            v.wait_ge(sem("dt_log"), 1)
            done(tt(dt_, dt_, t3, ALU.add), "dt_ready")
            done(stt(lg_, dt_, -1.0, eal[:].unsqueeze(1).to_broadcast([P, NT, 16]), ALU.mult, ALU.mult), "dt_ready")
            for t in range(NT):
                v.wait_ge(sem("xs_turned"), t + 1)
                cp(xs[:, t, :], ps[3])
                done(cp(Bt[:, t, :], ps[4][:, 0:P]), "xs_read")
            v.wait_ge(sem("sdec_exp"), 1)
            done(tt(wt, t3, dt_, ALU.mult), "v_chain")

            def split(ap):
                return ap.rearrange("p (h n) -> p h n", n=SHD)

            used = [1, 1, 2, 3, 4, 5, 5, 6, 7, 8]
            got = 0
            for n, (d, t) in enumerate(STEPS):
                if n >= 2:
                    v.wait_ge(sem("su_done"), used[n - 2])
                done(tt(split(vw[:, n % 2]), split(xs[:, t]), heads(wt[:, t, 8 * d:8 * d + 8]), ALU.mult), "svw")
                if t == 0:
                    continue
                v.wait_ge(sem("su_done"), got + 1)
                if t == 1:
                    done(cp(SS[:, d, d * (NL - 1), :], ps[6][:, 0:256]), "su_read")
                else:
                    c = t - NCX
                    to = SS[:, d, c + 1 - 2 * d, :]
                    for g in range(SG):
                        gs = slice(64 * g, 64 * g + 64)
                        done(tt(split(to[gs]), split(SS[gs, d, c, :]), heads(tot[gs, 0, c, 8 * d + 4 * g:8 * d + 4 * g + 4]), ALU.mult),
                             "v_chain")
                    done(tt(to, to, ps[6][:, 0:256], ALU.add), "su_read")
                got += 1
            for c in range(NL):
                t = NCX + c
                v.wait_ge(sem("su_done"), 8)
                for d in range(2):
                    done(tt(split(vw[:, d]), split(xs[:, t]), heads(dt_[:, t, 8 * d:8 * d + 8]), ALU.mult), "v_chain")
                v.wait_ge(sem("cb_done"), c + 1)
                for d in range(2):
                    for g in range(SG):
                        last = tt(CB[:, d, g], ps[3 + 3 * g][:, 0:P], (le, ge)[d], ALU.mult)
                done(last, "v_chain")
                for q4 in range(5):
                    if q4 < 4:
                        d, hf = q4 // 2, q4 % 2
                        m = 4 * c + q4
                        v.wait_ge(sem("se_done"), m + 1)
                        for h in range(4):
                            a = 8 * d + 4 * hf + h
                            last = ts(ES[:, d, 4 * hf + h, :], ps[4 + m % 2][:, h * P:(h + 1) * P], tot[:, 1, c, a:a + 1], 0.0,
                                      ALU.subtract, ALU.min)
                        done(last, "se_read")
                    if q4:
                        d, hf = (q4 - 1) // 2, (q4 - 1) % 2
                        v.wait_ge(sem("se_exp"), 4 * c + q4)
                        e = ES[:, d, 4 * hf:4 * hf + 4, :]
                        done(tt(e, e, CB[:, d, hf, :].unsqueeze(1).to_broadcast([P, 4, P]), ALU.mult), "sst")
                v.wait_ge(sem("sy_done"), c + 1)
                y0, y1 = ys[:, 0], ys[:, 1]
                for g in range(SG):
                    for d in range(2):
                        o = slice(256 * g, 256 * g + 256)
                        a = 8 * d + 4 * g
                        last = tt(split((y0, y1)[d][:, o]), split(ps[7 if g == 0 else 3][:, 256 * d:256 * d + 256]),
                                  heads(tot[:, 2, c, a:a + 4]), ALU.mult)
                done(last, "v_chain")
                done(tt(y0, y0, y1, ALU.add), "v_chain")
                done(tt(y0, y0, ps[6], ALU.add), "sy_read")
                done(tt(split(y1), split(xs[:, t]), heads(row["dsk"]), ALU.mult), "v_chain")
                done(tt(y0, y0, y1, ALU.add), "v_chain")
                v.wait_ge(sem("unit_read"), NU["z", c] + 1)
                done(tt(y0, y0, zz[:, c], ALU.mult), "y_gated")
                mean("y", slice(c, c + 1), SIN, c + 1)
                done(stt(y0, y0, ss[:, 1, c:c + 1], row["snorm"], ALU.mult, ALU.mult), "mix_ready")
                v.wait_ge(sem("mix_turned"), c + 1)
                done(cp(mixT[:, 0:4, c * P:(c + 1) * P], ps[4].rearrange("p (m t) -> p m t", m=4)), "mix_read")
            for c in range(NL):
                mean("o", slice(0, HH), HD, c + 1)
                for h in range(HH):
                    sl = slice(h * HD, (h + 1) * HD)
                    last = stt(osb[:, c, sl], osb[:, c, sl], ss[:, 1, h:h + 1], row["hnorm"][:, sl], ALU.mult, ALU.mult)
                done(last, "v_chain")
                done(tt(osb[:, c], osb[:, c], gg[:, c], ALU.mult), "mix_ready")
                v.wait_ge(sem("mix_turned"), NL + c + 1)
                for m in range(4):
                    last = cp(perm(mixT[:, 4 + m, :], c), ps[4 + c % 2][:, m * P:(m + 1) * P].rearrange("p (g r) -> p g r", r=ROWS))
                done(last, "mix_read")
            v.wait_ge(sem("post_in"), 64)
            done(tt(gw, gw, pst[:, 0:2], ALU.add), "v_chain")
            done(tt(gw, gw, pst[:, 2:4], ALU.mult), "v_chain")
            done(tt(mf[:], mf[:], colv[:, CC["adb"]][:, 24:40], ALU.add), "v_chain")
            done(stt(Af[:], mf[:, 8:16], 1.0, colv[:, CC["fpre"]], ALU.add, ALU.mult), "v_chain")
            v.wait_ge(sem("res_in"), 16)
            for c in range(NL):
                mean("m", slice(c, c + 1), D, c + 1)
                done(stt(mt[:, c], mt[:, c], ss[:, 1, c:c + 1], gw[:, 0], ALU.mult, ALU.mult), "v_chain")
                done(tt(x1[:, c], x1[:, c], mt[:, c], ALU.add), "x1_ready")
                mean("n", slice(c, c + 1), D, c + 1)
                done(ts(x1n[:, c], x1[:, c], ss[:, 1, c:c + 1], None, ALU.mult), "xn_ready")
                for h in range(2):
                    v.wait_ge(sem("hx_turned"), 2 * c + h + 1)
                    for m in range(4):
                        k = 4 * h + m
                        last = ts(hxT[:, c % 2, k, :], ps[5 + (2 * c + h) % 2][:, m * P:(m + 1) * P], Af[:, k:k + 1],
                                  mf[:, k:k + 1], ALU.mult, ALU.add)
                    done(last, "hx_read")
                v.wait_ge(sem("logit_done"), c + 1)
                done(tt(lg[:, c], ps[3][:, c * NE:(c + 1) * NE], row["rb"], ALU.add), "v_chain")
                done(nc.vector.max(out=top[:, c], in_=lg[:, c]), "v_chain")
                done(nc.vector.max_index(topi[:, c], top[:, c], lg[:, c]), "v_chain")
                done(cp(topf[:, c], topi[:, c]), "v_chain")
                for k in range(TOPK):
                    last = ts(OH[:, c, k], iota[:, 0:NE], topf[:, c, k:k + 1], None, ALU.is_equal)
                done(last, "v_chain")
            done(tt(M3[:], OH[:, :, 0], OH[:, :, 1], ALU.add), "v_chain")
            done(tt(M3[:], M3[:], OH[:, :, 2], ALU.add), "v_chain")
            done(tt(M3[:], M3[:], OH[:, :, 3], ALU.add), "chosen")
            rt_, rp_ = [rhsx[:, :, :, j].rearrange("p e c -> p c e") for j in range(2)]
            done(cp(rt_, heads(tokm, NE)), "v_chain")
            done(tt(rp_, OH[:, :, 1], heads(pairm, NE), ALU.add), "v_chain")
            for k in (2, 3):
                done(stt(rp_, OH[:, :, k], float(k), rp_, ALU.mult, ALU.add), "v_chain")
            done(tt(gate[:], top[:, :, 0:TOPK], top[:, :, 0:1].to_broadcast([P, NL, TOPK]), ALU.subtract), "top_sub")
            v.wait_ge(sem("top_exp"), 1)
            done(nc.vector.tensor_reduce(gsum[:].rearrange("p c a -> p (c a)"), gate[:], AX, ALU.add), "v_chain")
            done(nc.vector.reciprocal(gsum[:], gsum[:]), "v_chain")
            done(tt(gate[:], gate[:], gsum[:].to_broadcast([P, NL, TOPK]), ALU.mult), "v_chain")
            v.wait_ge(sem("rank_done"), 1)
            done(v.memset(rankb[:], -1.0), "v_chain")
            r0 = rankb[:, :, 0:NE]
            done(stt(r0, ps[4][:, 0:NL * NE].rearrange("p (c e) -> p c e", c=NL), 1.0, M3[:], ALU.add, ALU.mult), "v_chain")
            done(ts(r0, r0, 1.0, None, ALU.subtract), "v_chain")
            for b in range(1, MAXB):
                done(ts(rankb[:, :, b * NE:(b + 1) * NE], r0, float(P * b), None, ALU.subtract), "v_chain")
            done(nc.vector.tensor_reduce(cm[:, 0:1], ps[4][0:1, P:P + NE], AX, ALU.max), "v_chain")
            for b in range(1, MAXB):
                done(ts(cm[:, b:b + 1], cm[:, 0:1], float(P * b), float(NE), ALU.is_gt, ALU.mult), "v_chain")
            done(tt(cm[:, 1:2], cm[:, 1:2], cm[:, 2:3], ALU.add), "v_chain")
            done(tt(cm[:, 1:2], cm[:, 1:2], cm[:, 3:4], ALU.add), "v_chain")
            done(v.memset(xg, 0.0), "v_chain")
            done(ts(cnt_u[:], cm[:, 1:2], float(NE), None, ALU.add), "routed")
            blocks = v.value_load(cnt_u[0:1, 0:1], min_val=NE, max_val=NE * MAXB)

            def choose(n):
                cp(rsel[:], rhsx[:, bass.ds(n % NE, 1), :, :].rearrange("p a c w -> p (a c) w"))
                for c in range(NL):
                    last = ts(Pm[:, c, :], iota, rankb[:, c, bass.ds(n, 1)], None, ALU.is_equal)
                last.then_inc(sem("pm_ready"), 1)

            def number(n):
                v.wait_ge(sem("slots_done"), n + 1)
                ts(idx[:], ps[7][:, 0:2], NONE, None, ALU.add).then_inc(sem("idx_ready"), 1)

            v.sem_inc(sem("u_read"), 2)
            cp(rsel[:], rhsx[:, 0, :, :])
            for c in range(NL):
                last = ts(Pm[:, c, :], iota, rankb[:, c, 0:1], None, ALU.is_equal)
            last.then_inc(sem("pm_ready"), 1)
            number(0)
            with v.Fori(0, blocks) as i:
                v.wait_ge(sem("block_moved"), i + 1)
                v.wait_ge(sem("idx_ready"), i + 1)
                cp(idp[:], idx[:, 1:2]).then_inc(sem("idp_ready"), 1)
                v.wait_ge(sem("idp_ready"), i + 1)
                choose(i + 1)
                for hf in range(2):
                    v.wait_ge(sem(f"slot_free{4 * hf + 3}"), i + 2)
                    u = pall[:, 2 * hf:2 * hf + 2, :].rearrange("p b (n w) -> p b n w", w=2)
                    g3, l3 = [a[:, hf].rearrange("p (b n) -> p b n", b=2) for a in (glu, lin)]
                    ts(g3, u[:, :, :, 0], LIMIT, None, ALU.min).then_inc(sem("glu_ready"), 1)
                    ts(l3, u[:, :, :, 1], LIMIT, -LIMIT, ALU.min, ALU.max).then_inc(sem("u_read"), 1)
                    v.wait_ge(sem("glu_ready"), 2 * i + hf + 1)
                    v.wait_ge(sem("u_read"), 2 * i + hf + 3)
                    stt(lin[:, hf], lin[:, hf], 1.0, glu[:, hf], ALU.add, ALU.mult).then_inc(sem("lin_ready"), 1)
                    v.wait_ge(sem("lin_ready"), 2 * i + hf + 1)
                    v.wait_ge(sem("sg_ready"), 2 * i + hf + 1)
                    tt(actv[:, hf], lin[:, hf], sg[:, hf], ALU.mult).then_inc(sem("act_ready"), 1)
                    if hf == 0:
                        number(i + 1)
            for c in range(NL):
                v.wait_ge(sem(f"fin_in{c % 2}"), 32 * (c // 2 + 1))
                if c >= 2:
                    v.wait_ge(sem(f"out_done{c % 2}"), 16)
                o = fo[:, c % 2]
                done(ts(o, fin[:, c % 2, 0], gate[:, c, 0:1], None, ALU.mult), "v_chain")
                for k in range(1, TOPK):
                    done(stt(o, fin[:, c % 2, k], gate[:, c, k:k + 1], o, ALU.mult, ALU.add), "f_sum" if k == TOPK - 1 else "v_chain")
                mean("f", slice(c, c + 1), D, c + 1)
                done(stt(o, o, ss[:, 1, c:c + 1], gw[:, 1], ALU.mult, ALU.mult), "v_chain")
                done(tt(o, o, fx[:, c % 2], ALU.add), "out_ready")
                v.sem_inc(sem("fin_used"), 1)

        @block.gpsimd
        def _(pool):
            pool.wait_ge(sem("routed"), 1)
            blocks = pool.value_load(cnt_u[0:1, 0:1], min_val=NE, max_val=NE * MAXB)
            pool.sem_inc(sem("block_moved"), 1)

            def gather():
                pool.indirect_dma_start(xg, None, xn_d, bass.IndirectOffsetOnAxis(ap=idx[:, 0:1], axis=0),
                                        bounds_check=SEQ - 1, oob_is_err=False).then_inc(sem("xg_in"), 16)

            pool.wait_ge(sem("xn_out"), 16 * NL)
            pool.wait_ge(sem("idx_ready"), 1)
            gather()
            with pool.Fori(0, blocks) as i:
                pool.wait_ge(sem("idx_ready"), i + 2)
                pool.wait_ge(sem("xg_turned"), 2 * i + 2)
                pool.sem_inc(sem("gathering"), 1)
                gather()
                pool.wait_ge(sem("y_ready"), i + 2)
                pool.wait_ge(sem("idp_ready"), i + 1)
                pool.sem_inc(sem("scattering"), 1)
                pool.indirect_dma_start(yp_d, bass.IndirectOffsetOnAxis(ap=idp[:, 0:1], axis=0), yv, None,
                                        bounds_check=SEQ * TOPK - 1, oob_is_err=False).then_inc(sem("scattered"), 16)
                pool.wait_ge(sem("scattered"), 16 * i + 16)
                pool.wait_ge(sem("xg_in"), 16 * i + 32)
                pool.sem_inc(sem("block_moved"), 1)
            pool.sem_inc(sem("all_scattered"), 1)


def kernel(x, c, ctx, c_ctx, ada_w, ada_b, mix_pre_norm, mix_post_norm, w_in, w_out, ssd_conv_w, ssd_conv_b, ssd_dt_bias,
           ssd_a_log, ssd_d, ssd_norm, hg_lb, hg_norm, ffn_pre_norm, ffn_post_norm, router_w, router_b, moe_w1, moe_b1,
           moe_w2, moe_b2):
    import concourse.bacc as bacc
    from concourse.bass_utils import run_bass_kernel_spmd

    f = [np.asarray(a) for a in (c, c_ctx, mix_pre_norm, ffn_pre_norm, ssd_conv_w, ssd_conv_b, ada_b)]
    c_, cc_, mp, fp, cw, cb, ab = f

    def col(a):
        return np.ascontiguousarray(a.reshape(-1, P).T)

    cvec = np.stack([col(c_), col(cc_)], 2).reshape(P, 16)
    cwt = np.stack([col(cw[0, k]) for k in range(TAPS)], 2).reshape(P, 30)
    cols = np.ascontiguousarray(np.concatenate([cvec, col(mp), col(fp), cwt, col(cb), col(ab)], 1))
    ab = ab.reshape(-1)
    rows = np.concatenate([np.asarray(a).reshape(-1) for a in (
        hg_lb, ssd_norm, hg_norm, ssd_dt_bias, ssd_a_log, ssd_d, router_b, ab[2 * D:3 * D], ab[5 * D:6 * D],
        mix_post_norm, ffn_post_norm)])[None, :]
    bias = np.ascontiguousarray(np.concatenate([np.asarray(moe_b1)[0], np.asarray(moe_b2)[0]], 1))
    cf, cu = consts()
    arrays = dict(x=np.asarray(x)[0], ctx_in=np.asarray(ctx)[0], cols=cols, rows=np.ascontiguousarray(rows),
                  w_ada=np.asarray(ada_w)[0], w_in=np.asarray(w_in)[0], w_out=np.asarray(w_out)[0],
                  w_rt=np.asarray(router_w)[0], w1=np.asarray(moe_w1)[0], w2=np.asarray(moe_w2)[0], bb=bias, cf_in=cf, cu_in=cu)
    nc = bacc.Bacc("TRN2", target_bir_lowering=False, num_devices=1)
    args = {n: nc.dram_tensor(n, a.shape, mybir.dt.from_np(a.dtype), kind="ExternalInput").ap() for n, a in arrays.items()}
    out = nc.dram_tensor("out", (SEQ, D), F32, kind="ExternalOutput").ap()
    program(nc, out=out, **args)
    r = run_bass_kernel_spmd(nc, [arrays], core_ids=[0])
    return np.asarray(r.results[0]["out"]).reshape(1, SEQ, D)
```

```python
from contextlib import ExitStack

import numpy as np
import concourse.bass as bass
from concourse import mybir

F32 = mybir.dt.float32
BF16 = mybir.dt.bfloat16
U32 = mybir.dt.uint32
ALU = mybir.AluOpType
ACT = mybir.ActivationFunctionType
AX = mybir.AxisListType.X

P = 128
D = 1024
KD = D // P
SEQ, CTX = 512, 256
GRID_W = 64
ROWS = SEQ // GRID_W
NL, NCX = SEQ // P, CTX // P
NT = NL + NCX
SH, SHD, SST, SG = 8, 64, 64, 2
SIN = SH * SHD
TAPS = 5
XBC = SIN + 2 * SG * SST
HH, HD = 4, 128
HIN = HH * HD
NE, TOPK, DFF = 32, 4, 1024
ALPHA, LIMIT = 1.702, 7.0
EPS = 1e-6
MAXB = SEQ // P
NONE = 4096.0
SSD_COLS = SIN + XBC + 2 * SH
LEVELS = [64, 32, 16, 8, 4, 2, 1]
CONV = 2 + SEQ + 4 + CTX + 2
CW = CONV - 4
CX0 = SEQ + 4

COL = dict(z=(0, SIN), xs=(SIN, SIN), bcd=(2 * SIN, XBC - SIN + 2 * SH),
           q=(SSD_COLS, HIN), ff=(SSD_COLS + HIN, HIN), fb=(SSD_COLS + 2 * HIN, HIN),
           v=(SSD_COLS + 3 * HIN, HIN), g=(SSD_COLS + 4 * HIN, HIN))
LOADS = [("ada", j) for j in range(4)] + [(n, 0) for n in ("ff", "fb", "q", "v", "xs", "bcd")] + \
        [("ada", j) for j in range(4, 12)] + [("g", 0), ("z", 0), ("out", 0), ("out", 1)]
AT = {n: i for i, n in enumerate(LOADS)}

FIRST = [("ada", j) for j in range(4)]
MAIN = [(n, t) for n in ("ff", "fb") for t in range(NT)] + [("q", h) for h in range(HH)] + [("v", t) for t in range(NT)]
BACK1 = [(n, m) for m in range(4) for n in ("xl", "xc")] + [("bl", 0), ("bc", 0), ("cl", 0), ("dt", 0)]
BACK_G = [("g", t) for t in range(NL)]
BACK_Z = [("z", t) for t in range(NL)]
TAIL = [("ada", j) for j in range(4, 12)]
OUTS = [(n, t) for t in range(NL) for n in ("out0", "out1")]
UNITS = FIRST + MAIN + BACK1 + TAIL + BACK_G + BACK_Z + OUTS
NU = {u: i for i, u in enumerate(UNITS)}


def group(u):
    n = {"xl": "xs", "xc": "xs", "bl": "bcd", "bc": "bcd", "cl": "bcd", "dt": "bcd"}.get(u[0], u[0])
    return u if n == "ada" else ("out", int(n[3])) if n.startswith("out") else (n, 0)


LAST = {group(u): NU[u] for u in UNITS}

CC, _o = {}, 0
for _n, _w in (("c", 16), ("mpre", 8), ("fpre", 8), ("cw", 30), ("cb", 6), ("adb", 48)):
    CC[_n] = slice(_o, _o + _w)
    _o += _w
NCC = _o
RR, _o = {}, 0
for _n, _w in (("lbraw", 2048), ("snorm", 512), ("hnorm", 512), ("dtb", 16), ("alog", 16), ("dsk", 8), ("rb", 32),
               ("gbias", 2048), ("post", 2048)):
    RR[_n] = _o
    _o += _w
NRR = _o
NSM = RR["gbias"] - RR["snorm"]


def consts():
    a = np.arange(P)
    le = (a[:, None] <= a[None, :])
    mats = [np.eye(P), le, le.T, a[:, None] > a[None, :], a[:, None] < a[None, :], np.ones((P, P)),
            np.broadcast_to(a[None, :], (P, P))]
    f = np.concatenate([m.astype(np.float32) for m in mats], 1)
    tok = (np.arange(NL)[None, :] * P + a[:, None]).astype(np.float32)
    f = np.concatenate([f, tok - NONE, TOPK * tok - NONE], 1)
    m = []
    for s in LEVELS[1:]:
        b, half = a // (2 * s), (a // s) % 2
        m.append((b[:, None] == b[None, :]) & (half[:, None] != half[None, :]))
    m.append(np.eye(P, dtype=bool))
    return np.ascontiguousarray(f), np.ascontiguousarray(np.concatenate([x.astype(np.uint32) for x in m], 1))


NCF = 7 * P + 2 * NL


def program(nc, x, ctx_in, cols, rows, w_ada, w_in, w_out, w_rt, w1, w2, bb, cf_in, cu_in, out):
    with ExitStack() as es:
        sems = {}

        def sem(n):
            if n not in sems:
                sems[n] = es.enter_context(nc.semaphore(n))
            return sems[n]

        def sb(n, shape, dt=F32):
            return es.enter_context(nc.sbuf_tensor(n, shape, dt))

        cf = sb("cf", [P, NCF])
        cu = sb("cu", [P, 7, P], U32)
        ident, le, ge, gt, lt, ones, iota = [cf[:, i * P:(i + 1) * P] for i in range(7)]
        tokm = cf[:, 7 * P:7 * P + NL]
        pairm = cf[:, 7 * P + NL:7 * P + 2 * NL]
        colv = sb("colv", [P, NCC])
        rowv = sb("rowv", [P, NSM])
        row = {n: rowv[:, RR[n] - RR["snorm"]:RR[n] - RR["snorm"] + w] for n, w in
               (("snorm", 512), ("hnorm", 512), ("dtb", 16), ("alog", 16), ("dsk", 8), ("rb", 32))}
        sc = sb("sc", [P, KD, 2])
        mcol = sb("mcol", [P, 16, 2])
        mf = sb("mf", [P, 16])
        arow2 = sb("arow2", [1, 512])
        Am = sb("Am", [P, KD, 2])
        Af = sb("Af", [P, KD])
        ss = sb("ss", [P, 3, 8])
        dts = sb("dts", [P, 5, NT, 16])
        ea = sb("ea", [P, 2, NL, HH])
        tot = sb("tot", [P, 3, NL, 16])
        eal = sb("eal", [P, 16])

        ARENA = 48152
        arena = sb("arena", [P, ARENA])
        pos = [0]

        def take(n):
            a = pos[0]
            pos[0] += n
            assert pos[0] <= ARENA, pos
            return a

        def at(o, n, pat=None, **kw):
            v = arena[:, o:o + n]
            return v.rearrange(pat, **kw) if pat else v

        HT, W0, LA0, K0, CXR0 = take(KD * 768), take(8192), take(4096), take(4096), take(6 * CW)
        QV0, S0, T0, LB0, HN0 = take(5120), take(4096), take(5632), take(2048), take(4096)
        hT = at(HT, KD * 768, "p (k t) -> p k t", k=KD)
        hN = at(HN0, 4096, "p (k t) -> p k t", k=KD)
        gw = at(LB0, 2048, "p (a n) -> p a n", a=2)
        W = at(W0, 8192, "p (b k n) -> p b k n", b=2, k=KD)
        la = at(LA0, 4096, "p (d c n) -> p d c n", d=2, c=NL)
        kk = at(K0, 4096, "p (d c n) -> p d c n", d=2, c=NL)
        lac = at(CXR0, 2048, "p (d c n) -> p d c n", d=2, c=NCX)
        kc = at(CXR0 + 2048, 2048, "p (d c n) -> p d c n", d=2, c=NCX)
        cv = at(CXR0, 6 * CW, "p (m n) -> p m n", m=6)
        qT = at(QV0, 2048, "p (h t) -> p h t", h=HH)
        vv = at(QV0 + 2048, 3072, "p (c n) -> p c n", c=NT)
        HS = at(S0, 4096, "p (d c n) -> p d c n", d=2, c=NL)
        Gs = at(T0, 1024, "p (d h t) -> p d h t", d=2, h=HH)
        eG = at(T0 + 1024, 1024, "p (d h t) -> p d h t", d=2, h=HH)
        kT = at(T0 + 2048, 1024, "p (d h t) -> p d h t", d=2, h=HH)
        EE = at(T0 + 3072, 2048, "p (b w h t) -> p b w h t", b=2, w=2, h=HH)
        scr = at(T0 + 5120, 512, "p (h t) -> p h t", h=HH)
        raw = at(LB0, 2 * CONV, "p (b n) -> p b n", b=2)
        lbr = at(LB0, 1024, "p (d n) -> p d n", d=2)
        oml = at(LB0 + 1024, 1024, "p (d n) -> p d n", d=2)
        xt = at(S0, 2048, "p (b n) -> p b n", b=2)
        junk = at(T0 + 3072, 1024)
        lbraw = at(T0, 2048)
        arow = at(T0 + 4096, 1024, "p (b n) -> p b n", b=2)[0:2]
        tk = at(T0, 1024, "p (b n) -> p b n", b=2)
        osb = la[:, 0]
        zz = at(LA0 + 2048, 2048, "p (c n) -> p c n", c=NL)
        gg = at(K0, 2048, "p (c n) -> p c n", c=NL)
        SS = at(K0 + 2048, 2048, "p (d c n) -> p d c n", d=2, c=NL)
        xs = at(S0, 3072, "p (t n) -> p t n", t=NT)
        Bt = at(S0 + 3072, 768, "p (t n) -> p t n", t=NT)
        vw = at(T0, 1024, "p (b n) -> p b n", b=2)
        CB = at(T0 + 1024, 512, "p (d g t) -> p d g t", d=2, g=SG)
        ES = at(T0 + 1536, 2048, "p (d h t) -> p d h t", d=2, h=SH)
        ys = at(T0 + 3584, 1024, "p (b n) -> p b n", b=2)
        yt = at(T0 + 5120, 512)
        junk2 = at(T0 + 4608, 1024)
        mixT = at(QV0, 4096, "p (k t) -> p k t", k=KD)
        mt = at(S0, 4096, "p (c n) -> p c n", c=NL)
        x1 = at(LA0, 4096, "p (c n) -> p c n", c=NL)
        pst = at(K0, 4096, "p (a n) -> p a n", a=4)
        x1n = at(K0, 4096, "p (c n) -> p c n", c=NL)
        hxT = at(T0, 2048, "p (b k t) -> p b k t", b=2, k=KD)
        bsrc = at(LA0, 3072)
        bparts = at(K0, 4608).bitcast(BF16).rearrange("p (r n) -> p r n", r=3)
        wr = at(0, 12 * 2048, "p (s k n) -> p s k n", s=12, k=2)
        M0 = 12 * 2048
        xg = at(M0, 1024)
        xgT = at(M0 + 1024, 1024, "p (k t) -> p k t", k=KD)
        glu, lin, sg, actv = [at(M0 + 2048 + 1024 * j, 1024, "p (f n) -> p f n", f=2) for j in range(4)]
        aT = at(M0 + 6144, 1024, "p (k t) -> p k t", k=KD)
        yv = at(M0 + 7168, 1024)
        Pm = at(M0 + 8192, 512, "p (c t) -> p c t", c=NL)
        bpt = at(M0 + 8704, 1536).bitcast(BF16)
        fin = at(0, 16384, "p (b k n) -> p b k n", b=NL, k=TOPK)
        fo = at(16384, 2048, "p (b n) -> p b n", b=2)
        fx = at(HN0, 4096, "p (b n) -> p b n", b=NL)
        assert M0 + 8704 + 1536 <= HN0
        rankb = at(T0 + 2560, NL * NE * (MAXB + 1), "p (c n) -> p c n", c=NL)
        M3 = at(T0 + 3456, NL * NE, "p (c e) -> p c e", c=NL)
        OH = at(T0 + 2048, NL * TOPK * NE, "p (c k e) -> p c k e", c=NL, k=TOPK)
        lg = at(T0 + 3584, NL * NE, "p (c e) -> p c e", c=NL)
        rt = at(T0 + 3712, KD * NE, "p (k e) -> p k e", k=KD)
        top = sb("top", [P, NL, 8])
        topi = sb("topi", [P, NL, 8], U32)
        topf = at(T0 + 3968, NL * 8, "p (c k) -> p c k", c=NL)
        rhsx = at(T0 + 3200, NE * NL * 2, "p (e c w) -> p e c w", e=NE, c=NL)
        rsel = sb("rsel", [P, NL, 2])
        gate = sb("gate", [P, NL, TOPK])
        gsum = sb("gsum", [P, NL, 1])
        cm = at(T0 + 4000, 4)[0:1]
        cnt_u = sb("cnt_u", [1, 1], U32)
        idx = sb("idx", [P, 2], U32)
        idp = sb("idp", [P, 1], U32)
        ones3 = sb("ones3", [3, P], BF16)

        pall = es.enter_context(nc.psum_tensor("pall", [P, 8, 512], F32))
        ps = [pall[:, b, :] for b in range(8)]

        xn_d = nc.dram_tensor("xn_d", (SEQ, D), F32, kind="Internal").ap()
        x1_d = nc.dram_tensor("x1_d", (SEQ, D), F32, kind="Internal").ap()
        yp_d = nc.dram_tensor("yp_d", (SEQ * TOPK, D), F32, kind="Internal").ap()
        ada_d = nc.dram_tensor("ada_d", (8, 512), F32, kind="Internal").ap()
        bp_d = nc.dram_tensor("bp_d", (3, NE, 3 * D), BF16, kind="Internal").ap()

        def perm(ap, c=None):
            v = ap.rearrange("p (r g) -> p g r", g=GRID_W)
            n = GRID_W // NL
            return v if c is None else v[:, c * n:(c + 1) * n, :]

        def heads(ap, w=64):
            return ap.unsqueeze(2).to_broadcast([ap.shape[0], ap.shape[1], w])

        def chained(eng):
            n = {}

            def done(ins, s):
                ins.then_inc(sem(s), 1)
                n[s] = n.get(s, 0) + 1
                eng.wait_ge(sem(s), n[s])
            return done

        HSTEPS = [(d, s if d == 0 else NL - 1 - s) for s in range(NL - 1) for d in range(2)]
        STEPS = [(0, 0), (0, 1), (1, 0), (1, 1)] + [s for t in range(NL - 1) for s in ((0, NCX + t), (1, NT - 1 - t))]
        MIXES = [(k, c) for c in range(NL) for k in "oy"]
        slots1 = {}
        _b = BACK1 + TAIL + BACK_G
        for c in range(NL):
            for L in range(7):
                if _b:
                    slots1[c, L] = _b.pop(0)

        block = es.enter_context(nc.Block())

        @block.sync
        def _(sp):
            nc.sync.dma_start(cf[:], cf_in).then_inc(sem("consts_in"), 16)
            nc.sync.dma_start(colv[:], cols).then_inc(sem("consts_in"), 16)

            def load_x(t):
                if t >= 2:
                    sp.wait_ge(sem("x_turned"), 2 * (t - 1))
                src = ctx_in[t * P:(t + 1) * P, :] if t < NCX else x[(t - NCX) * P:(t - NCX + 1) * P, :]
                nc.sync.dma_start(xt[:, t % 2, :], src).then_inc(sem(f"x_in{t % 2}"), 16)

            def load(i):
                name, j = LOADS[i]
                if i >= 2:
                    sp.wait_ge(sem("unit_done"), LAST[LOADS[i - 2]] + 1)
                if name == "ada":
                    src = w_ada[:, j * 512:(j + 1) * 512]
                elif name == "out":
                    src = w_out[:, j * 512:(j + 1) * 512]
                else:
                    src = w_in[:, COL[name][0]:COL[name][0] + COL[name][1]]
                nc.sync.dma_start(W[:, i % 2, :, 0:src.shape[1]],
                                  src.rearrange("(k p) n -> p k n", p=P)).then_inc(sem(f"w_in{i % 2}"), 16)
                if i >= 2 and LOADS[i - 2] in TAIL:
                    p = LOADS[i - 2][1] - 4
                    sp.wait_ge(sem("unit_read"), NU[LOADS[i - 2]] + 1)
                    nc.sync.dma_start(ada_d[p:p + 1, :], arow2[:]).then_inc(sem("ada_out"), 16)

            load_x(0)
            load_x(1)
            load(0)
            load_x(2)
            load_x(3)
            load(1)
            load_x(4)
            load_x(5)
            o = RR["snorm"]
            nc.sync.dma_start(bsrc[0:NE, :], bb).then_inc(sem("bias_src"), 16)
            nc.sync.dma_start(lbraw, rows[:, 0:2048].to_broadcast([P, 2048])).then_inc(sem("rows_in"), 16)
            load(2)
            load(3)
            nc.sync.dma_start(cu[:], cu_in.rearrange("p (m t) -> p m t", m=7)).then_inc(sem("rows_in"), 16)
            nc.sync.dma_start(rowv[:], rows[:, o:o + NSM].to_broadcast([P, NSM])).then_inc(sem("rows_in"), 16)
            load(4)
            load(5)
            sp.wait_ge(sem("bias_split"), 5)
            for r in range(3):
                nc.sync.dma_start(bp_d[r], bparts[0:NE, r, :]).then_inc(sem("bias_stored"), 16)
            for i in range(6, len(LOADS)):
                load(i)
            sp.wait_ge(sem("mix_read"), 2 * NL)
            sp.wait_ge(sem("ada_out"), 16 * len(TAIL))
            nc.sync.dma_start(mf[:], ada_d.rearrange("a b -> (a b)")[D:3 * D].rearrange("(m p) -> p m", p=P),
                              allow_slow_non_contiguous=True).then_inc(sem("post_in"), 16)
            for h in range(2):
                nc.sync.dma_start(gw[:, h, :], ada_d.rearrange("a (q b) -> q (a b)", q=1)[:, 3 * D * h:3 * D * h + D].to_broadcast([P, D]))\
                  .then_inc(sem("post_in"), 16)
            nc.sync.dma_start(rt, w_rt.rearrange("(k p) e -> p k e", p=P)).then_inc(sem("post_in"), 16)
            o = RR["gbias"]
            nc.sync.dma_start(pst, rows[:, o:o + 4096].rearrange("a (b n) -> a b n", b=4).to_broadcast([P, 4, D]))\
              .then_inc(sem("post_in"), 16)
            nc.sync.dma_start(x1, x.rearrange("(c p) n -> p c n", p=P)).then_inc(sem("res_in"), 16)
            def load_slot(s, e):
                if s < 8:
                    h, k = s // 4, s % 4
                    src = w1[e, k * 256:(k + 1) * 256, h * 1024:(h + 1) * 1024]
                else:
                    src = w2[e, (s - 8) * 256:(s - 7) * 256, :]
                nc.sync.dma_start(wr[:, s], src.rearrange("a (k p) n -> p (a k) n", p=P)).then_inc(sem(f"slot_in{s}"), 16)

            EARLY = KD * 768 // 2048
            EARLY2 = EARLY + 8192 // 2048
            sp.wait_ge(sem("unit_done"), NU["z", NL - 1] + 1)
            for s in range(EARLY):
                load_slot(s, slice(0, 1))
            for c in range(NL):
                sp.wait_ge(sem("x1_ready"), c + 1)
                nc.sync.dma_start(x1_d[c * P:(c + 1) * P, :], x1[:, c, :]).then_inc(sem("x1_out"), 16)
                sp.wait_ge(sem("xn_ready"), c + 1)
                nc.sync.dma_start(xn_d[c * P:(c + 1) * P, :], x1n[:, c, :]).then_inc(sem("xn_out"), 16)
                if c == NL - 2:
                    sp.wait_ge(sem("unit_done"), len(UNITS))
                    for s in range(EARLY, EARLY2):
                        load_slot(s, slice(0, 1))
            sp.wait_ge(sem("routed"), 1)
            sp.wait_ge(sem("x1_out"), 16 * NL)
            sp.wait_ge(sem("xn_out"), 16 * NL)
            sp.wait_ge(sem("bias_stored"), 48)
            blocks = sp.value_load(cnt_u[0:1, 0:1], min_val=NE, max_val=NE * MAXB)

            def load_rest(e, i):
                for s in range(EARLY2, 12):
                    sp.wait_ge(sem(f"slot_free{s}"), i)
                    load_slot(s, e)
                    if s == 7:
                        sp.wait_ge(sem("bias_free"), i)
                        nc.sync.dma_start(bpt[0:3, :], bp_d[:, e, :].rearrange("r a n -> r (a n)")).then_inc(sem("bias_in"), 16)

            with sp.Fori(1, blocks) as i:
                load_rest(bass.ds((i - 1) % NE, 1), i)
                for s in range(EARLY2):
                    sp.wait_ge(sem(f"slot_free{s}"), i + 1)
                    load_slot(s, bass.ds(i % NE, 1))
            load_rest(slice(NE - 1, NE), blocks)
            nc.sync.dma_start(fx, x1_d.rearrange("(c p) n -> p c n", p=P)).then_inc(sem("res_in"), 16)
            sp.wait_ge(sem("all_scattered"), 1)
            for c in range(NL):
                nc.sync.dma_start(fin[:, c], yp_d[c * P * TOPK:(c + 1) * P * TOPK, :].rearrange("(p k) n -> p k n", k=TOPK))\
                  .then_inc(sem(f"fin_in{c}"), 16)
            for c in range(NL):
                if c >= 1:
                    sp.wait_ge(sem("out_ready"), c)
                    nc.sync.dma_start(out[(c - 1) * P:c * P, :], fo[:, (c - 1) % 2]).then_inc(sem(f"out_done{(c - 1) % 2}"), 16)
            sp.wait_ge(sem("out_ready"), NL)
            nc.sync.dma_start(out[(NL - 1) * P:NL * P, :], fo[:, (NL - 1) % 2]).then_inc(sem(f"out_done{(NL - 1) % 2}"), 16)
            sp.wait_ge(sem("out_done0"), 32)
            sp.wait_ge(sem("out_done1"), 32)

        @block.tensor
        def _(pe):
            mm = nc.tensor.matmul
            tp = nc.tensor.transpose

            def unit(u):
                name, j = u
                i = AT[group(u)]
                pe.wait_ge(sem(f"w_in{i % 2}"), 16 * (i // 2 + 1))
                if NU[u] >= 3:
                    pe.wait_ge(sem("unit_read"), NU[u] - 2)
                if u == ("xl", 0):
                    pe.wait_ge(sem("hn_mod"), 1)
                w, b = W[:, i % 2], ps[NU[u] % 3]
                if name == "dt":
                    for t in range(NT):
                        for k in range(KD):
                            lhs = hT[:, k, t * P:(t + 1) * P] if t < NCX else hN[:, k, (t - NCX) * P:(t - NCX + 1) * P]
                            last = mm(b[:, t * 16:(t + 1) * 16], lhs, w[:, k, 256:272],
                                      start=k == 0, stop=k == KD - 1)
                    last.then_inc(sem("unit_done"), 1)
                    return
                for k in range(KD):
                    if name == "ada":
                        o, lhs, rhs = b[0:2, :], sc[:, k, :], w[:, k, :]
                    elif name in ("ff", "fb", "v", "g"):
                        a = CTX + j * P if j < NL else (j - NL) * P
                        lhs = hT[:, k, a:a + P]
                        o, rhs = b, w[:, k, :]
                    elif name == "z":
                        o, lhs, rhs = b, hN[:, k, j * P:(j + 1) * P], w[:, k, :]
                    elif name == "q":
                        o, lhs, rhs = b, w[:, k, j * P:(j + 1) * P], hT[:, k, CTX:CTX + SEQ]
                    elif name in ("xl", "bl", "cl"):
                        a = dict(x=j * P, b=0, c=P)[name[0]]
                        o, lhs, rhs = b, w[:, k, a:a + P], hN[:, k, :]
                    elif name in ("xc", "bc"):
                        a = dict(x=j * P, b=0)[name[0]]
                        o, lhs, rhs = b[:, 0:CTX], w[:, k, a:a + P], hT[:, k, 0:CTX]
                    else:
                        o, lhs, rhs = b, mixT[:, k, j * P:(j + 1) * P], w[:, k, :]
                    last = mm(o, lhs, rhs, start=k == 0, stop=k == KD - 1)
                last.then_inc(sem("unit_done"), 1)

            def ada_turn(j):
                pe.wait_ge(sem("unit_read"), NU["ada", j] + 1)
                if j:
                    pe.wait_ge(sem("arow_read"), j)
                for m in range(4):
                    last = tp(ps[3][:, 2 * m:2 * m + 2], arow[0:2, j % 2, m * P:(m + 1) * P], ident[0:2, 0:2])
                last.then_inc(sem("arow_turned"), 1)

            pe.wait_ge(sem("consts_in"), 32)

            def turn_x(t):
                pe.wait_ge(sem("x_normed"), t + 1)
                for h in range(2):
                    n = 2 * t + h
                    if n >= 2:
                        pe.wait_ge(sem("h_read"), n - 1)
                    if n - 2 >= 2 * NCX:
                        pe.wait_ge(sem("hp_read"), n - 1 - 2 * NCX)
                    for m in range(4):
                        last = tp(ps[5 + n % 2][:, m * P:(m + 1) * P], xt[:, t % 2, (4 * h + m) * P:(4 * h + m + 1) * P], ident)
                    last.then_inc(sem("x_turned"), 1)

            turn_x(0)
            turn_x(1)
            pe.wait_ge(sem("sc_ready"), 1)
            unit(("ada", 0))
            turn_x(2)
            turn_x(3)
            unit(("ada", 1))
            ada_turn(0)
            turn_x(4)
            turn_x(5)
            unit(("ada", 2))
            ada_turn(1)
            unit(("ada", 3))
            ada_turn(2)
            ada_turn(3)
            pe.wait_ge(sem("h_mod"), 1)
            for u in MAIN:
                unit(u)

            pe.wait_ge(sem("la_ready"), 2)
            n = 0
            for d in range(2):
                for t in range(NCX):
                    if n:
                        pe.wait_ge(sem("hd_exp"), n)
                    far = 1 - t if t == d else None
                    last = mm(ps[3], (gt, lt)[d], lac[:, d, t, :], start=True, stop=far is None)
                    if far is not None:
                        last = mm(ps[3], ones, lac[:, d, far, :], start=False, stop=True)
                    last.then_inc(sem("hd_done"), 1)
                    n += 1
                pe.wait_ge(sem("hkw"), n)
                for h in range(HH):
                    sl = slice(h * HD, (h + 1) * HD)
                    for t in range(NCX):
                        last = mm(ps[4 + d][:, sl], kc[:, d, t, sl], vv[:, NL + t, sl], start=t == 0, stop=t == NCX - 1)
                last.then_inc(sem("hctx_done"), 1)
            pe.wait_ge(sem("hctx_read"), 2)
            for m, (d, c) in enumerate(HSTEPS):
                pe.wait_ge(sem("hd_exp"), n)
                mm(ps[3], (gt, lt)[d], la[:, d, c, :], start=True, stop=True).then_inc(sem("hd_done"), 1)
                n += 1
                if m:
                    pe.wait_ge(sem("hea"), m)
                for h in range(HH):
                    last = mm(ps[5][:, h:h + 1], la[:, d, c, h * HD:(h + 1) * HD], ones[:, 0:1], start=True, stop=True)
                last.then_inc(sem("hea_done"), 1)
                pe.wait_ge(sem("hkw"), n)
                if m:
                    pe.wait_ge(sem("hu_read"), m)
                for h in range(HH):
                    sl = slice(h * HD, (h + 1) * HD)
                    last = mm(ps[4][:, sl], tk[:, m % 2, sl], vv[:, c, sl], start=True, stop=True)
                last.then_inc(sem("hu_done"), 1)
            pe.wait_ge(sem("hu_read"), len(HSTEPS))
            pe.wait_ge(sem("hea"), len(HSTEPS))
            lv = 0
            def sums(c):
                if c:
                    pe.wait_ge(sem("g_read"), 2 * c)
                for d in range(2):
                    for h in range(HH):
                        sl = slice(h * HD, (h + 1) * HD)
                        last = mm(ps[3 + d][:, sl], la[:, d, c, sl], (le, ge)[d], start=True, stop=True)
                    last.then_inc(sem("g_done"), 1)

            sums(0)
            for c in range(NL):
                if c:
                    pe.wait_ge(sem("level_read"), 8 * c)
                for d in range(2):
                    for h in range(HH):
                        last = tp(ps[5 + d][:, h * P:(h + 1) * P], kk[:, d, c, h * HD:(h + 1) * HD], ident)
                    last.then_inc(sem("kt_done"), 1)
                pe.wait_ge(sem("kt_read"), 2 * (c + 1))
                for L in range(8):
                    pe.wait_ge(sem("level_ready"), lv + 1)
                    if lv >= 2:
                        pe.wait_ge(sem("level_read"), lv - 1)
                    for h in range(HH):
                        rhs = EE[:, lv % 2, 0, h, :] if L < 7 else qT[:, h, c * P:(c + 1) * P]
                        last = mm(ps[5 + lv % 2][:, h * P:(h + 1) * P], EE[:, lv % 2, 1, h, :], rhs, start=True, stop=True)
                    last.then_inc(sem("level_done"), 1)
                    lv += 1
                    if (c, L) in slots1:
                        unit(slots1[c, L])
                    if L == 5 and c + 1 < NL:
                        sums(c + 1)
                pe.wait_ge(sem("level_read"), lv)
                if c:
                    pe.wait_ge(sem("ho_read"), c)
                for h in range(HH):
                    sl = slice(h * HD, (h + 1) * HD)
                    mm(ps[7][:, sl], scr[:, h, :], vv[:, c, sl], start=True, stop=False)
                    mm(ps[7][:, sl], eG[:, 0, h, :], HS[:, 0, c, sl], start=False, stop=False)
                    last = mm(ps[7][:, sl], eG[:, 1, h, :], HS[:, 1, c, sl], start=False, stop=True)
                last.then_inc(sem("ho_done"), 1)

            pe.wait_ge(sem("ho_read"), NL)
            pe.wait_ge(sem("dt_ready"), 2)
            LG = dts[:, 1]
            for d in range(2):
                sl = slice(8 * d, 8 * d + 8)
                mm(ps[7][:, 48 * d:48 * d + 48].rearrange("p (t n) -> p t n", n=8), (gt, lt)[d], LG[:, :, sl], start=True, stop=False)
                mm(ps[7][:, 48 * d + 8 * d:48 * d + 8 * d + 8], ones, LG[:, 1 - d, sl], start=False, stop=True)
                mm(ps[7][:, 256 + 32 * d:288 + 32 * d].rearrange("p (c n) -> p c n", n=8), (le, ge)[d], LG[:, NCX:, sl],
                   start=True, stop=True)
            mm(ps[7][:, 128:192].rearrange("p (c n) -> p c n", n=16), ones, LG[:, NCX:, :], start=True, stop=True)\
              .then_inc(sem("sdec_done"), 1)
            pe.wait_ge(sem("cv_ready"), 6)
            for t in range(NT):
                o = CX0 + t * P if t < NCX else (t - NCX) * P
                if t >= 2:
                    pe.wait_ge(sem("xs_read"), t - 1)
                for m in range(5):
                    b = ps[3 + 2 * (t % 2)][:, m * P:(m + 1) * P] if m < 4 else ps[4 + 2 * (t % 2)][:, 0:P]
                    last = tp(b, cv[:, m, o:o + P], ident)
                last.then_inc(sem("xs_turned"), 1)
            back = list(BACK_Z)
            pe.wait_ge(sem("xs_read"), NT)
            done = 0
            for n, (d, t) in enumerate(STEPS):
                if t == 0:
                    continue
                pe.wait_ge(sem("svw"), n + 1)
                if done >= 2:
                    pe.wait_ge(sem("su_read"), done - 1)
                for g in range(SG):
                    o = ps[6 + d][64 * g:64 * g + 64, 0:256]
                    sl, sv = slice(64 * g, 64 * g + 64), slice(256 * g, 256 * g + 256)
                    if t == 1:
                        mm(o, Bt[:, 0, sl], vw[:, (n - 1) % 2, sv], start=True, stop=False)
                        last = mm(o, Bt[:, 1, sl], vw[:, n % 2, sv], start=False, stop=True)
                    else:
                        last = mm(o, Bt[:, t, sl], vw[:, n % 2, sv], start=True, stop=True)
                last.then_inc(sem("su_done"), 1)
                done += 1
                if t > 1 and back:
                    unit(back.pop(0))
            assert not back
            pe.wait_ge(sem("su_read"), done)
            BT, CT = cv[:, 4], cv[:, 5]

            def decays(c, q4):
                d, hf = q4 // 2, q4 % 2
                m = 4 * c + q4
                if m >= 2:
                    pe.wait_ge(sem("se_read"), m - 1)
                for h in range(4):
                    a = 8 * d + 4 * hf + h
                    last = mm(ps[4 + m % 2][:, h * P:(h + 1) * P], LG[:, NCX + c, a:a + 1].to_broadcast([P, P]), (le, ge)[d],
                              start=True, stop=True)
                last.then_inc(sem("se_done"), 1)

            def turn_out(n):
                k, c = MIXES[n]
                pe.wait_ge(sem("mix_ready"), n + 1)
                if n >= 2:
                    pe.wait_ge(sem("mix_read"), n - 1)
                src = osb[:, c] if k == "o" else ys[:, c % 2]
                for m in range(4):
                    last = tp(ps[n % 2][:, m * P:(m + 1) * P], src[:, m * P:(m + 1) * P], ident)
                last.then_inc(sem("mix_turned"), 1)

            pe.wait_ge(sem("unit_read"), NU[BACK_Z[-1]] + 1)
            for c in range(NL):
                sl = slice(c * P, (c + 1) * P)
                decays(c, 0)
                decays(c, 1)
                if c:
                    pe.wait_ge(sem("sy_read"), c)
                for g in range(SG):
                    gs = slice(64 * g, 64 * g + 64)
                    last = mm(ps[3 + 3 * g][:, 0:P], BT[gs, sl], CT[gs, sl], start=True, stop=True)
                last.then_inc(sem("cb_done"), 1)
                decays(c, 2)
                decays(c, 3)
                pe.wait_ge(sem("sst"), 4 * c + 4)
                for h in range(SH):
                    for d in range(2):
                        last = mm(ps[6][:, h * 64:(h + 1) * 64], ES[:, d, h, :], vw[:, d, h * 64:(h + 1) * 64],
                                  start=d == 0, stop=d == 1)
                for g in range(SG):
                    gs = slice(64 * g, 64 * g + 64)
                    for d in range(2):
                        last = mm(ps[7 if g == 0 else 3][:, 256 * d:256 * d + 256], CT[gs, sl], SS[gs, d, c, :], start=True, stop=True)
                last.then_inc(sem("sy_done"), 1)
                for n in range(max(2 * c - 1, 0), 2 * c + 1):
                    turn_out(n)
            turn_out(2 * NL - 1)
            pe.wait_ge(sem("mix_read"), 2 * NL)
            outs = list(OUTS)
            for _ in range(4):
                unit(outs.pop(0))
            pe.wait_ge(sem("post_in"), 80)
            for c in range(NL):
                for _ in range(min(2, len(outs))):
                    unit(outs.pop(0))
                pe.wait_ge(sem("xn_ready"), c + 1)
                for h in range(2):
                    n = 2 * c + h
                    if n >= 2:
                        pe.wait_ge(sem("hx_read"), n - 1)
                    for m in range(4):
                        last = tp(ps[5 + n % 2][:, m * P:(m + 1) * P], x1n[:, c, (4 * h + m) * P:(4 * h + m + 1) * P], ident)
                    last.then_inc(sem("hx_turned"), 1)
                pe.wait_ge(sem("hx_read"), 2 * (c + 1))
                for k in range(KD):
                    last = mm(ps[3][:, c * NE:(c + 1) * NE], hxT[:, c % 2, k, :], rt[:, k, :], start=k == 0, stop=k == KD - 1)
                last.then_inc(sem("logit_done"), 1)
            pe.wait_ge(sem("chosen"), 1)
            for c in range(NL):
                for b in range(c + 1):
                    mm(ps[4][:, c * NE:(c + 1) * NE], lt if b == c else ones, M3[:, b, :], start=b == 0, stop=b == c)
            for b in range(NL):
                last = mm(ps[4][:, P:P + NE], ones, M3[:, b, :], start=b == 0, stop=b == NL - 1)
            last.then_inc(sem("rank_done"), 1)

            pe.wait_ge(sem("routed"), 1)
            blocks = pe.value_load(cnt_u[0:1, 0:1], min_val=NE, max_val=NE * MAXB)
            for s in range(12):
                pe.sem_inc(sem(f"slot_free{s}"), 1)
            pe.sem_inc(sem("bias_free"), 1)

            def find_slots():
                for c in range(NL):
                    last = mm(ps[7][:, 0:2], Pm[:, c, :], rsel[:, c, :], start=c == 0, stop=c == NL - 1)
                last.then_inc(sem("slots_done"), 1)

            def turn_rows(h):
                for m in range(4):
                    last = tp(ps[6 + h][:, m * P:(m + 1) * P], xg[:, (4 * h + m) * P:(4 * h + m + 1) * P], ident)
                last.then_inc(sem("xg_turned"), 1)

            pe.wait_ge(sem("pm_ready"), 1)
            find_slots()
            pe.wait_ge(sem("xg_in"), 16)
            turn_rows(0)
            turn_rows(1)
            with pe.Fori(0, blocks) as i:
                pe.wait_ge(sem("xgT_ready"), 2 * i + 2)
                pe.wait_ge(sem("bias_in"), 16 * i + 16)
                for hf in range(2):
                    pe.wait_ge(sem("u_read"), 2 * i + hf + 1)
                    for n2 in range(2):
                        o = hf * 1024 + n2 * 512
                        mm(ps[2 * hf + n2], ones3[:], bpt[0:3, o:o + 512], start=True, stop=False)
                    for s in range(4):
                        pe.wait_ge(sem(f"slot_in{4 * hf + s}"), 16 * i + 16)
                        for k2 in range(2):
                            for n2 in range(2):
                                k = 2 * s + k2
                                last = mm(ps[2 * hf + n2], xgT[:, k, :], wr[:, 4 * hf + s, k2, n2 * 512:(n2 + 1) * 512],
                                          start=False, stop=k == KD - 1)
                        last.then_inc(sem(f"slot_free{4 * hf + s}"), 1)
                        if hf == 1 and s == 2:
                            pe.wait_ge(sem("act_ready"), 2 * i + 1)
                            for m in range(4):
                                last = tp(ps[6][:, m * P:(m + 1) * P], actv[:, 0, m * P:(m + 1) * P], ident)
                            last.then_inc(sem("act_turned"), 1)
                    if hf == 0:
                        pe.wait_ge(sem("pm_ready"), i + 2)
                        find_slots()
                pe.wait_ge(sem("y_ready"), i + 1)
                for n2 in range(2):
                    last = mm(ps[4 + n2], ones3[:], bpt[0:3, 2048 + n2 * 512:2560 + n2 * 512], start=True, stop=False)
                last.then_inc(sem("bias_free"), 1)
                for hf in range(2):
                    if hf == 1:
                        pe.wait_ge(sem("act_ready"), 2 * i + 2)
                        pe.wait_ge(sem("idx_ready"), i + 2)
                        for m in range(4):
                            last = tp(ps[7][:, m * P:(m + 1) * P], actv[:, 1, m * P:(m + 1) * P], ident)
                        last.then_inc(sem("act_turned"), 1)
                        pe.wait_ge(sem("xg_in"), 16 * i + 32)
                        turn_rows(0)
                    pe.wait_ge(sem("aT_ready"), 2 * i + hf + 1)
                    if hf == 1:
                        turn_rows(1)
                    for s in range(2 * hf, 2 * hf + 2):
                        pe.wait_ge(sem(f"slot_in{8 + s}"), 16 * i + 16)
                        for k2 in range(2):
                            for n2 in range(2):
                                k = 2 * s + k2
                                last = mm(ps[4 + n2], aT[:, k, :], wr[:, 8 + s, k2, n2 * 512:(n2 + 1) * 512],
                                          start=False, stop=k == KD - 1)
                        last.then_inc(sem(f"slot_free{8 + s}"), 1)

        @block.scalar
        def _(act):
            A = nc.scalar.activation
            done = chained(act)

            act.wait_ge(sem("consts_in"), 32)
            A(sc[:].rearrange("p k s -> p (k s)"), colv[:, CC["c"]], ACT.Silu).then_inc(sem("sc_ready"), 1)

            def read(u):
                name, j = u
                act.wait_ge(sem("unit_done"), NU[u] + 1)
                b = ps[NU[u] % 3]
                if name == "ada":
                    if j >= 4:
                        if j > 4:
                            act.wait_ge(sem("ada_out"), 16 * (j - 4))
                        i = A(arow2[:], b[0:1, :], ACT.Copy)
                    else:
                        if j >= 2:
                            act.wait_ge(sem("arow_turned"), j - 1)
                        i = A(arow[:, j % 2, :], b[0:2, :], ACT.Copy)
                elif name in ("ff", "fb"):
                    d = int(name == "fb")
                    i = A(kk[:, d, j, :] if j < NL else kc[:, d, j - NL, :], b, ACT.Sigmoid)
                elif name == "q":
                    i = A(qT[:, j, :], b, ACT.Silu)
                elif name == "v":
                    i = A(vv[:, j, :], b, ACT.Copy)
                elif name in ("xl", "bl", "cl", "xc", "bc"):
                    m = dict(x=j, b=4, c=5)[name[0]]
                    if m >= 2:
                        act.wait_ge(sem("conv_done"), m - 1)
                    else:
                        act.wait_ge(sem("raw_zeroed"), 1)
                    i = A(raw[:, m % 2, 2:2 + SEQ], b, ACT.Copy) if name[1] == "l" else \
                        A(raw[:, m % 2, 6 + SEQ:6 + SEQ + CTX], b[:, 0:CTX], ACT.Copy)
                elif name == "dt":
                    i = A(dts[:, 0].rearrange("p t n -> p (t n)"), b[:, 0:NT * 16], ACT.Copy)
                elif name == "g":
                    i = A(gg[:, j, :], b, ACT.Silu)
                elif name == "z":
                    i = A(zz[:, j, :], b, ACT.Silu)
                else:
                    i = A(mt[:, j, (name == "out1") * 512:(name == "out1") * 512 + 512], b, ACT.Copy)
                i.then_inc(sem("unit_read"), 1)

            def square_x(t):
                act.wait_ge(sem(f"x_in{t % 2}"), 16 * (t // 2 + 1))
                done(A(junk, xt[:, t % 2, :], ACT.Square, accum_out=ss[:, 0, t:t + 1]), "x_sq")
                act.wait_ge(sem("x_ms"), t + 1)
                A(ss[:, 2, t:t + 1], ss[:, 1, t:t + 1], ACT.Sqrt).then_inc(sem("x_rt"), 1)

            def order_x(t):
                for h in range(2):
                    n, c = 2 * t + h, t - NCX
                    act.wait_ge(sem("h_read"), n + 1)
                    to = hT[:, 4 * h:4 * h + 4, CTX:CTX + SEQ].rearrange("p k (g r) -> p k r g", r=ROWS)
                    src = ps[5 + n % 2].rearrange("p (k r g) -> p k r g", k=4, r=2)
                    for r in range(2):
                        last = A(to[:, :, 2 * c + r, :], src[:, :, r, :], ACT.Copy)
                    last.then_inc(sem("hp_read"), 1)

            square_x(0)
            square_x(1)
            for t in range(NCX, NT):
                square_x(t)
                if t > NCX:
                    order_x(t - 1)
                if t == 3:
                    read(("ada", 0))
                if t == 5:
                    read(("ada", 1))
            order_x(NT - 1)
            read(("ada", 2))
            read(("ada", 3))
            act.wait_ge(sem("lb_diff"), 1)
            A(lbr.rearrange("p d n -> p (d n)"), lbraw[:, 0:1024], ACT.Sigmoid).then_inc(sem("sc_ready"), 1)
            act.wait_ge(sem("am_ready"), 1)
            act.wait_ge(sem("h_read"), 2 * NT)
            for k in range(KD):
                last = A(hN[:, k, :], hN[:, k, :], ACT.Identity, bias=mcol[:, k, 0:1], scale=Am[:, k, 0:1])
            last.then_inc(sem("hn_mod"), 1)
            act.wait_ge(sem("bias_stored"), 48)
            for u in MAIN:
                read(u)
            act.wait_ge(sem("f_ready"), 2 * NT)
            A(at(LA0, 4096), at(LA0, 4096), ACT.Ln).then_inc(sem("la_ready"), 1)
            A(at(CXR0, 2048), at(CXR0, 2048), ACT.Ln).then_inc(sem("la_ready"), 1)
            n = 0
            for _ in range(2 * NCX):
                if n >= 2:
                    act.wait_ge(sem("hkw"), n - 1)
                act.wait_ge(sem("hd_done"), n + 1)
                A(tk[:, n % 2, :], ps[3], ACT.Exp).then_inc(sem("hd_exp"), 1)
                n += 1
            for m, (d, c) in enumerate(HSTEPS):
                act.wait_ge(sem("hkw"), min(n - 1, 2 * NCX))
                if m >= 2:
                    act.wait_ge(sem("hu_done"), m - 1)
                act.wait_ge(sem("hd_done"), n + 1)
                A(tk[:, n % 2, :], ps[3], ACT.Exp).then_inc(sem("hd_exp"), 1)
                n += 1
                act.wait_ge(sem("hea_done"), m + 1)
                A(ea[:, d, c, :], ps[5][:, 0:HH], ACT.Exp).then_inc(sem("hea"), 1)
            t3 = dts[:, 3]

            def sums(c):
                if c:
                    act.wait_ge(sem("e_sub"), 7 * c)
                for d in range(2):
                    act.wait_ge(sem("g_done"), 2 * c + d + 1)
                    A(Gs[:, d].rearrange("p h t -> p (h t)"), ps[3 + d], ACT.Copy).then_inc(sem("g_copied"), 1)

            def level(c, L):
                act.wait_ge(sem("e_sub"), 7 * c + L + 1)
                e = EE[:, (8 * c + L) % 2].rearrange("p w h t -> p (w h t)")
                A(e, e, ACT.Exp).then_inc(sem("e_exp"), 1)

            sums(0)
            level(0, 0)
            for c in range(NL):
                for d in range(2):
                    A(eG[:, d].rearrange("p h t -> p (h t)"), ps[3 + d], ACT.Exp).then_inc(sem("g_read"), 1)

                for L in range(8):
                    if L + 1 < 7:
                        level(c, L + 1)
                    if (c, L) in slots1:
                        read(slots1[c, L])
                    if c == 2 and L < 6:
                        act.wait_ge(sem("conv_done"), L + 1)
                        A(cv[:, L], cv[:, L], ACT.Silu).then_inc(sem("cv_ready"), 1)
                if c == 1:
                    act.wait_ge(sem("dt_abs"), 1)
                    done(A(t3, t3, ACT.Exp, scale=-1.0), "dt_log")
                    done(A(t3, t3, ACT.Ln, bias=1.0), "dt_log")
                    A(eal[:], row["alog"], ACT.Exp).then_inc(sem("dt_log"), 1)
                if c + 1 < NL:
                    sums(c + 1)
                    level(c + 1, 0)
                act.wait_ge(sem("ho_done"), c + 1)
                A(osb[:, c, :], ps[7], ACT.Copy).then_inc(sem("ho_read"), 1)
            act.wait_ge(sem("sdec_done"), 1)
            for d in range(2):
                A(t3[:, :, 8 * d:8 * d + 8], ps[7][:, 48 * d:48 * d + 48].rearrange("p (t n) -> p t n", n=8), ACT.Exp)
                src = ps[7][:, 256 + 32 * d:288 + 32 * d].rearrange("p (c n) -> p c n", n=8)
                A(tot[:, 1, :, 8 * d:8 * d + 8], src, ACT.Copy)
                A(tot[:, 2, :, 8 * d:8 * d + 8], src, ACT.Exp)
            A(tot[:, 0].rearrange("p c n -> p (c n)"), ps[7][:, 128:192], ACT.Exp).then_inc(sem("sdec_exp"), 1)
            for u in BACK_Z:
                read(u)
            for c in range(NL + 1):
                if c < NL:
                    for q4 in range(4):
                        d, hf = q4 // 2, q4 % 2
                        act.wait_ge(sem("se_read"), 4 * c + q4 + 1)
                        e = ES[:, d, 4 * hf:4 * hf + 4, :].rearrange("p h t -> p (h t)")
                        A(e, e, ACT.Exp).then_inc(sem("se_exp"), 1)
                if c:
                    act.wait_ge(sem("y_gated"), c)
                    done(A(junk2[:, 0:SIN], ys[:, (c - 1) % 2], ACT.Square, accum_out=ss[:, 0, 3 + c:4 + c]), "y_sq")
                    act.wait_ge(sem("y_ms"), c)
                    A(ss[:, 2, 3 + c:4 + c], ss[:, 1, 3 + c:4 + c], ACT.Sqrt).then_inc(sem("y_rt"), 1)
                if c < NL:
                    if c:
                        act.wait_ge(sem("mix_ready"), 2 * c - 1)
                    for h in range(HH):
                        sl = slice(h * HD, (h + 1) * HD)
                        done(A(junk2[:, sl], osb[:, c, sl], ACT.Square, accum_out=ss[:, 0, h:h + 1]), "o_sq")
                    act.wait_ge(sem("o_ms"), c + 1)
                    A(ss[:, 2, 0:HH], ss[:, 1, 0:HH], ACT.Sqrt).then_inc(sem("o_rt"), 1)
            outs = list(OUTS)
            read(outs.pop(0))
            read(outs.pop(0))
            for c in range(NL):
                for s, src in (("m", mt), ("n", x1)):
                    if s == "m":
                        act.wait_ge(sem("unit_read"), NU["out1", c] + 1)
                    if s == "n":
                        act.wait_ge(sem("x1_ready"), c + 1)
                    done(A(junk2, src[:, c, :], ACT.Square, accum_out=ss[:, 0, c:c + 1]), f"{s}_sq")
                    act.wait_ge(sem(f"{s}_ms"), c + 1)
                    A(ss[:, 2, c:c + 1], ss[:, 1, c:c + 1], ACT.Sqrt).then_inc(sem(f"{s}_rt"), 1)
                    if s == "m" and outs:
                        read(outs.pop(0))
                        read(outs.pop(0))
            act.wait_ge(sem("top_sub"), 1)
            A(gate[:].rearrange("p c k -> p (c k)"), gate[:].rearrange("p c k -> p (c k)"), ACT.Exp).then_inc(sem("top_exp"), 1)
            act.wait_ge(sem("routed"), 1)
            blocks = act.value_load(cnt_u[0:1, 0:1], min_val=NE, max_val=NE * MAXB)
            act.sem_inc(sem("y_ready"), 1)

            def spread(h):
                for m in range(4):
                    k = 4 * h + m
                    last = A(xgT[:, k, :], ps[6 + h][:, m * P:(m + 1) * P], ACT.Identity, bias=mf[:, k:k + 1], scale=Af[:, k:k + 1])
                last.then_inc(sem("xgT_ready"), 1)

            for h in range(2):
                act.wait_ge(sem("xg_turned"), h + 1)
                spread(h)
            with act.Fori(0, blocks) as i:
                for hf in range(2):
                    act.wait_ge(sem("glu_ready"), 2 * i + hf + 1)
                    A(sg[:, hf, :], glu[:, hf, :], ACT.Sigmoid, scale=ALPHA).then_inc(sem("sg_ready"), 1)
                    act.wait_ge(sem("act_turned"), 2 * i + hf + 1)
                    A(aT[:, 4 * hf:4 * hf + 4, :].rearrange("p k t -> p (k t)"), ps[6 + hf], ACT.Copy).then_inc(sem("aT_ready"), 1)
                for h in range(2):
                    act.wait_ge(sem("xg_turned"), 2 * i + h + 3)
                    spread(h)
                act.wait_ge(sem("slot_free11"), i + 2)
                act.wait_ge(sem("block_moved"), i + 1)
                A(yv, pall[:, 4:6, :].rearrange("p b n -> p (b n)"), ACT.Copy).then_inc(sem("y_ready"), 1)
            for c in range(NL):
                act.wait_ge(sem("f_sum"), c + 1)
                done(A(junk2, fo[:, c % 2], ACT.Square, accum_out=ss[:, 0, c:c + 1]), "f_sq")
                act.wait_ge(sem("f_ms"), c + 1)
                A(ss[:, 2, c:c + 1], ss[:, 1, c:c + 1], ACT.Sqrt).then_inc(sem("f_rt"), 1)

        @block.vector
        def _(v):
            tt, ts, stt, cp = nc.vector.tensor_tensor, nc.vector.tensor_scalar, nc.vector.scalar_tensor_tensor, nc.vector.tensor_copy
            done = chained(v)

            def mean(s, col, width, count):
                v.wait_ge(sem(f"{s}_sq"), count * (col.stop - col.start if s == "o" else 1))
                done(ts(ss[:, 1, col], ss[:, 0, col], 1.0 / width, EPS, ALU.mult, ALU.add), f"{s}_ms")
                v.wait_ge(sem(f"{s}_rt"), count)
                done(nc.vector.reciprocal(ss[:, 1, col], ss[:, 2, col]), "v_chain")

            v.memset(ones3[:], 1.0)

            def modulation(j):
                v.wait_ge(sem("arow_turned"), j + 1)
                s = slice(4 * j, 4 * j + 4)
                adb = colv[:, CC["adb"]][:, s]
                done(tt(mcol[:, s, :], ps[3][:, 0:8].rearrange("p (m s) -> p m s", s=2), heads(adb, 2), ALU.add), "arow_read")

            def norm_x(t):
                mean("x", slice(t, t + 1), D, t + 1)
                done(ts(xt[:, t % 2, :], xt[:, t % 2, :], ss[:, 1, t:t + 1], None, ALU.mult), "x_normed")

            def store_x(t):
                for h in range(2):
                    v.wait_ge(sem("x_turned"), 2 * t + h + 1)
                    ks = slice(4 * h, 4 * h + 4)
                    to = hT[:, ks, t * P:(t + 1) * P] if t < NCX else hN[:, ks, (t - NCX) * P:(t - NCX + 1) * P]
                    done(cp(to, ps[5 + (2 * t + h) % 2].rearrange("p (k t) -> p k t", k=4)), "h_read")

            for t in range(NT + 1):
                if t < NT:
                    norm_x(t)
                if t:
                    store_x(t - 1)
            v.wait_ge(sem("bias_src"), 16)
            b = bsrc[0:NE, :]
            for r in range(3):
                done(cp(bparts[0:NE, r, :], b), "bias_split")
                if r < 2:
                    done(tt(b, b, bparts[0:NE, r, :], ALU.subtract), "bias_split")
            v.wait_ge(sem("rows_in"), 48)
            done(tt(lbraw[:, 0:1024], lbraw[:, 0:1024], lbraw[:, 1024:2048], ALU.subtract), "lb_diff")

            for j in range(4):
                modulation(j)
            v.wait_ge(sem("consts_in"), 32)
            done(stt(Am[:], mcol[:, 8:16, :], 1.0, heads(colv[:, CC["mpre"]], 2), ALU.add, ALU.mult), "am_ready")
            v.wait_ge(sem("hp_read"), 2 * NL)
            for k in range(KD):
                for s, o in ((1, hT[:, k, 0:CTX]), (0, hT[:, k, CTX:CTX + SEQ])):
                    last = ts(o, o, Am[:, k, s:s + 1], mcol[:, k, s:s + 1], ALU.mult, ALU.add)
            last.then_inc(sem("h_mod"), 1)
            v.wait_ge(sem("sc_ready"), 2)
            done(ts(oml, lbr, -1.0, 1.0, ALU.mult, ALU.add), "v_chain")
            for u in MAIN:
                if u[0] in ("ff", "fb"):
                    d, j = int(u[0] == "fb"), u[1]
                    v.wait_ge(sem("unit_read"), NU[u] + 1)
                    if j == 0:
                        v.wait_ge(sem("bias_stored"), 48)
                    kd, ld = (kk[:, d, j], la[:, d, j]) if j < NL else (kc[:, d, j - NL], lac[:, d, j - NL])
                    done(tt(ld, kd, oml[:, d], ALU.mult), "v_chain")
                    done(tt(ld, ld, lbr[:, d], ALU.add), "v_chain")
                    done(ts(kd, ld, -1.0, 1.0, ALU.mult, ALU.add), "f_ready")
                elif u[0] == "q":
                    v.wait_ge(sem("unit_read"), NU[u] + 1)
                    done(ts(qT[:, u[1]], qT[:, u[1]], HD ** -0.5, None, ALU.mult), "v_chain")
            done(v.memset(raw, 0.0), "raw_zeroed")
            n = 0
            for d in range(2):
                for t in range(NCX):
                    v.wait_ge(sem("hd_exp"), n + 1)
                    done(tt(kc[:, d, t], kc[:, d, t], tk[:, n % 2], ALU.mult), "hkw")
                    n += 1
                v.wait_ge(sem("hctx_done"), d + 1)
                done(cp(HS[:, d, d * (NL - 1)], ps[4 + d]), "hctx_read")
            for m, (d, c) in enumerate(HSTEPS):
                v.wait_ge(sem("hd_exp"), n + 1)
                done(tt(tk[:, n % 2], tk[:, n % 2], kk[:, d, c], ALU.mult), "hkw")
                n += 1
                v.wait_ge(sem("hea"), m + 1)
                v.wait_ge(sem("hu_done"), m + 1)
                for h in range(HH):
                    sl = slice(h * HD, (h + 1) * HD)
                    last = stt(HS[:, d, c + 1 - 2 * d, sl], HS[:, d, c, sl], ea[:, d, c, h:h + 1], ps[4][:, sl], ALU.mult, ALU.add)
                done(last, "hu_read")
            lv = 0
            ready = {("xc", m): m for m in range(4)}
            ready.update({("bc", 0): 4, ("cl", 0): 5})

            def conv(m):
                cw, cb = colv[:, CC["cw"]], colv[:, CC["cb"]]
                r = raw[:, m % 2]
                done(ts(cv[:, m, :], r[:, 0:CW], cw[:, 5 * m:5 * m + 1], cb[:, m:m + 1], ALU.mult, ALU.add), "v_chain")
                for k in range(1, TAPS):
                    done(stt(cv[:, m, :], r[:, k:k + CW], cw[:, 5 * m + k:5 * m + k + 1], cv[:, m, :], ALU.mult, ALU.add),
                         "conv_done" if k == TAPS - 1 else "v_chain")

            for c in range(NL):
                cs = slice(c * P, (c + 1) * P)

                def halves(t, s):
                    w = t.rearrange("p h (b w s) -> p (h b) w s", w=2, s=s)
                    return w[:, :, 0, :], w[:, :, 1, :]

                def subtract(L, lv):
                    s = LEVELS[L]
                    if lv >= 2:
                        v.wait_ge(sem("level_done"), lv - 1)
                    gfl, gfr = halves(Gs[:, 0], s)
                    gbl, gbr = halves(Gs[:, 1], s)
                    ql, qr = halves(EE[:, lv % 2, 0], s)
                    kl, kr = halves(EE[:, lv % 2, 1], s)
                    sh = list(gfl.shape)
                    mf, mb = gfl[:, :, s - 1:s].to_broadcast(sh), gbr[:, :, 0:1].to_broadcast(sh)
                    tt(qr, gfr, mf, ALU.subtract)
                    tt(ql, gbl, mb, ALU.subtract)
                    tt(kl, mf, gfl, ALU.subtract)
                    tt(kr, mb, gbr, ALU.subtract).then_inc(sem("e_sub"), 1)

                def multiply(L, lv):
                    s = LEVELS[L]
                    v.wait_ge(sem("e_exp"), 7 * c + L + 1)
                    kl, kr = halves(EE[:, lv % 2, 1], s)
                    fl, _ = halves(kT[:, 0], s)
                    _, br = halves(kT[:, 1], s)
                    tt(EE[:, lv % 2, 0], EE[:, lv % 2, 0], qT[:, :, cs], ALU.mult)
                    tt(kl, kl, fl, ALU.mult)
                    tt(kr, kr, br, ALU.mult).then_inc(sem("level_ready"), 1)

                def keep(L, lv):
                    v.wait_ge(sem("level_done"), lv + 1)
                    src = ps[5 + lv % 2].rearrange("p (h t) -> p h t", h=HH)
                    if L == 0:
                        ins = cp(scr, src)
                    else:
                        ins = nc.vector.copy_predicated(scr, cu[:, L - 1, :].unsqueeze(1).to_broadcast([P, HH, P]), src)
                    done(ins, "level_read")

                v.wait_ge(sem("g_copied"), 2 * (c + 1))
                subtract(0, lv)
                if c:
                    keep(7, lv - 1)
                for d in range(2):
                    v.wait_ge(sem("kt_done"), 2 * c + d + 1)
                    done(cp(kT[:, d].rearrange("p h t -> p (h t)"), ps[5 + d]), "kt_read")
                for L in range(8):
                    if L + 1 < 7:
                        subtract(L + 1, lv + 1)
                    if L < 7:
                        multiply(L, lv)
                    else:
                        v.wait_ge(sem("level_done"), lv - 1)
                        tt(EE[:, lv % 2, 1], kT[:, 0], kT[:, 1], ALU.add).then_inc(sem("level_ready"), 1)
                    if L == 1 and c:
                        v.wait_ge(sem("ho_done"), c)
                    if L:
                        keep(L - 1, lv - 1)
                    if L == 1:
                        for d in range(2):
                            v.wait_ge(sem("g_read"), 2 * c + d + 1)
                            done(tt(eG[:, d], eG[:, d], qT[:, :, cs], ALU.mult), "v_chain")
                    if (c, L - 1) in slots1 and slots1[c, L - 1] in ready:
                        v.wait_ge(sem("unit_read"), NU[slots1[c, L - 1]] + 1)
                        conv(ready[slots1[c, L - 1]])
                    lv += 1
                r0, lg_, dt_, t3, wt = [dts[:, j] for j in range(5)]
                if c == 1:
                    v.wait_ge(sem("unit_read"), NU["dt", 0] + 1)
                    done(tt(r0, r0, row["dtb"].unsqueeze(1).to_broadcast([P, NT, 16]), ALU.add), "v_chain")
                    done(stt(t3, r0, -1.0, r0, ALU.mult, ALU.max), "dt_abs")
                    done(ts(dt_, r0, 0.0, None, ALU.max), "v_chain")
                if c == 2:
                    v.wait_ge(sem("dt_log"), 3)
                    done(tt(dt_, dt_, t3, ALU.add), "dt_ready")
                    done(stt(lg_, dt_, -1.0, eal[:].unsqueeze(1).to_broadcast([P, NT, 16]), ALU.mult, ALU.mult), "dt_ready")
            keep(7, lv - 1)
            for t in range(NT):
                v.wait_ge(sem("xs_turned"), t + 1)
                cp(xs[:, t, :], ps[3 + 2 * (t % 2)])
                done(cp(Bt[:, t, :], ps[4 + 2 * (t % 2)][:, 0:P]), "xs_read")
            v.wait_ge(sem("sdec_exp"), 1)
            done(tt(wt, t3, dt_, ALU.mult), "v_chain")

            def split(ap):
                return ap.rearrange("p (h n) -> p h n", n=SHD)

            used = [1, 1, 2, 2, 3, 4, 5, 6, 7, 8]

            def weigh(n):
                d, t = STEPS[n]
                if n >= 2:
                    v.wait_ge(sem("su_done"), used[n - 2])
                done(tt(split(vw[:, n % 2]), split(xs[:, t]), heads(wt[:, t, 8 * d:8 * d + 8]), ALU.mult), "svw")

            weigh(0)
            weigh(1)
            got = 0
            for n, (d, t) in enumerate(STEPS):
                if n >= 1 and n + 1 < len(STEPS):
                    weigh(n + 1)
                if t == 0:
                    continue
                v.wait_ge(sem("su_done"), got + 1)
                if t == 1:
                    done(cp(SS[:, d, d * (NL - 1), :], ps[6 + d][:, 0:256]), "su_read")
                else:
                    c = t - NCX
                    to = SS[:, d, c + 1 - 2 * d, :]
                    for g in range(SG):
                        gs = slice(64 * g, 64 * g + 64)
                        last = tt(split(to[gs]), split(SS[gs, d, c, :]), heads(tot[gs, 0, c, 8 * d + 4 * g:8 * d + 4 * g + 4]), ALU.mult)
                    done(last, "v_chain")
                    done(tt(to, to, ps[6 + d][:, 0:256], ALU.add), "su_read")
                got += 1

            def finish_y(c):
                y = ys[:, c % 2]
                done(tt(split(yt), split(xs[:, NCX + c]), heads(row["dsk"]), ALU.mult), "v_chain")
                done(tt(y, y, yt, ALU.add), "v_chain")
                v.wait_ge(sem("unit_read"), NU["z", c] + 1)
                done(tt(y, y, zz[:, c], ALU.mult), "y_gated")
                mean("y", slice(4 + c, 5 + c), SIN, c + 1)
                done(stt(y, y, ss[:, 1, 4 + c:5 + c], row["snorm"], ALU.mult, ALU.mult), "mix_ready")

            def finish_o(c):
                mean("o", slice(0, HH), HD, c + 1)
                for h in range(HH):
                    sl = slice(h * HD, (h + 1) * HD)
                    last = stt(osb[:, c, sl], osb[:, c, sl], ss[:, 1, h:h + 1], row["hnorm"][:, sl], ALU.mult, ALU.mult)
                done(last, "v_chain")
                v.wait_ge(sem("unit_read"), NU["g", c] + 1)
                done(tt(osb[:, c], osb[:, c], gg[:, c], ALU.mult), "mix_ready")

            def store_out(n):
                k, c = MIXES[n]
                v.wait_ge(sem("mix_turned"), n + 1)
                if k == "y":
                    last = cp(mixT[:, 0:4, c * P:(c + 1) * P], ps[n % 2].rearrange("p (m t) -> p m t", m=4))
                else:
                    for m in range(4):
                        last = cp(perm(mixT[:, 4 + m, :], c), ps[n % 2][:, m * P:(m + 1) * P].rearrange("p (g r) -> p g r", r=ROWS))
                done(last, "mix_read")

            v.wait_ge(sem("su_done"), 8)
            for c in range(NL + 1):
                if c < NL:
                    t = NCX + c
                    for q4 in range(5):
                        if q4 < 4:
                            d, hf = q4 // 2, q4 % 2
                            m = 4 * c + q4
                            v.wait_ge(sem("se_done"), m + 1)
                            for h in range(4):
                                a = 8 * d + 4 * hf + h
                                last = ts(ES[:, d, 4 * hf + h, :], ps[4 + m % 2][:, h * P:(h + 1) * P], tot[:, 1, c, a:a + 1], 0.0,
                                          ALU.subtract, ALU.min)
                            done(last, "se_read")
                        if q4 == 0:
                            v.wait_ge(sem("cb_done"), c + 1)
                            for d in range(2):
                                for g in range(SG):
                                    last = tt(CB[:, d, g], ps[3 + 3 * g][:, 0:P], (le, ge)[d], ALU.mult)
                            done(last, "v_chain")
                        else:
                            d, hf = (q4 - 1) // 2, (q4 - 1) % 2
                            if hf == 0:
                                done(tt(split(vw[:, d]), split(xs[:, t]), heads(dt_[:, t, 8 * d:8 * d + 8]), ALU.mult), "v_chain")
                            v.wait_ge(sem("se_exp"), 4 * c + q4)
                            e = ES[:, d, 4 * hf:4 * hf + 4, :]
                            done(tt(e, e, CB[:, d, hf, :].unsqueeze(1).to_broadcast([P, 4, P]), ALU.mult), "sst")
                if c:
                    finish_y(c - 1)
                if c < NL:
                    finish_o(c)
                    v.wait_ge(sem("sy_done"), c + 1)
                    if c >= 2:
                        v.wait_ge(sem("mix_turned"), 2 * c - 2)
                    y = ys[:, c % 2]
                    for g in range(SG):
                        for d in range(2):
                            o = slice(256 * g, 256 * g + 256)
                            a = 8 * d + 4 * g
                            last = tt(split((y, yt)[d][:, o]), split(ps[7 if g == 0 else 3][:, 256 * d:256 * d + 256]),
                                      heads(tot[:, 2, c, a:a + 4]), ALU.mult)
                    done(last, "v_chain")
                    done(tt(y, y, yt, ALU.add), "v_chain")
                    done(tt(y, y, ps[6], ALU.add), "sy_read")
                    for n in range(max(2 * c - 1, 0), 2 * c + 1):
                        store_out(n)
            store_out(2 * NL - 1)
            v.wait_ge(sem("post_in"), 80)
            done(tt(gw, gw, pst[:, 0:2], ALU.add), "v_chain")
            done(tt(gw, gw, pst[:, 2:4], ALU.mult), "v_chain")
            done(tt(mf[:], mf[:], colv[:, CC["adb"]][:, 24:40], ALU.add), "v_chain")
            done(stt(Af[:], mf[:, 8:16], 1.0, colv[:, CC["fpre"]], ALU.add, ALU.mult), "v_chain")
            v.wait_ge(sem("res_in"), 16)
            for c in range(NL):
                mean("m", slice(c, c + 1), D, c + 1)
                done(stt(mt[:, c], mt[:, c], ss[:, 1, c:c + 1], gw[:, 0], ALU.mult, ALU.mult), "v_chain")
                done(tt(x1[:, c], x1[:, c], mt[:, c], ALU.add), "x1_ready")
                mean("n", slice(c, c + 1), D, c + 1)
                done(ts(x1n[:, c], x1[:, c], ss[:, 1, c:c + 1], None, ALU.mult), "xn_ready")
                for h in range(2):
                    v.wait_ge(sem("hx_turned"), 2 * c + h + 1)
                    for m in range(4):
                        k = 4 * h + m
                        last = ts(hxT[:, c % 2, k, :], ps[5 + (2 * c + h) % 2][:, m * P:(m + 1) * P], Af[:, k:k + 1],
                                  mf[:, k:k + 1], ALU.mult, ALU.add)
                    done(last, "hx_read")
                v.wait_ge(sem("logit_done"), c + 1)
                done(tt(lg[:, c], ps[3][:, c * NE:(c + 1) * NE], row["rb"], ALU.add), "v_chain")
                done(nc.vector.max(out=top[:, c], in_=lg[:, c]), "v_chain")
                done(nc.vector.max_index(topi[:, c], top[:, c], lg[:, c]), "v_chain")
                done(cp(topf[:, c], topi[:, c]), "v_chain")
                for k in range(TOPK):
                    last = ts(OH[:, c, k], iota[:, 0:NE], topf[:, c, k:k + 1], None, ALU.is_equal)
                done(last, "v_chain")
            done(tt(M3[:], OH[:, :, 0], OH[:, :, 1], ALU.add), "v_chain")
            done(tt(M3[:], M3[:], OH[:, :, 2], ALU.add), "v_chain")
            done(tt(M3[:], M3[:], OH[:, :, 3], ALU.add), "chosen")
            rt_, rp_ = [rhsx[:, :, :, j].rearrange("p e c -> p c e") for j in range(2)]
            done(cp(rt_, heads(tokm, NE)), "v_chain")
            done(tt(rp_, OH[:, :, 1], heads(pairm, NE), ALU.add), "v_chain")
            for k in (2, 3):
                done(stt(rp_, OH[:, :, k], float(k), rp_, ALU.mult, ALU.add), "v_chain")
            done(tt(gate[:], top[:, :, 0:TOPK], top[:, :, 0:1].to_broadcast([P, NL, TOPK]), ALU.subtract), "top_sub")
            v.wait_ge(sem("top_exp"), 1)
            done(nc.vector.tensor_reduce(gsum[:].rearrange("p c a -> p (c a)"), gate[:], AX, ALU.add), "v_chain")
            done(nc.vector.reciprocal(gsum[:], gsum[:]), "v_chain")
            done(tt(gate[:], gate[:], gsum[:].to_broadcast([P, NL, TOPK]), ALU.mult), "v_chain")
            v.wait_ge(sem("rank_done"), 1)
            done(v.memset(rankb[:], -1.0), "v_chain")
            r0 = rankb[:, :, 0:NE]
            done(stt(r0, ps[4][:, 0:NL * NE].rearrange("p (c e) -> p c e", c=NL), 1.0, M3[:], ALU.add, ALU.mult), "v_chain")
            done(ts(r0, r0, 1.0, None, ALU.subtract), "v_chain")
            for b in range(1, MAXB):
                done(ts(rankb[:, :, b * NE:(b + 1) * NE], r0, float(P * b), None, ALU.subtract), "v_chain")
            done(nc.vector.tensor_reduce(cm[:, 0:1], ps[4][0:1, P:P + NE], AX, ALU.max), "v_chain")
            for b in range(1, MAXB):
                done(ts(cm[:, b:b + 1], cm[:, 0:1], float(P * b), float(NE), ALU.is_gt, ALU.mult), "v_chain")
            done(tt(cm[:, 1:2], cm[:, 1:2], cm[:, 2:3], ALU.add), "v_chain")
            done(tt(cm[:, 1:2], cm[:, 1:2], cm[:, 3:4], ALU.add), "v_chain")
            done(v.memset(xg, 0.0), "v_chain")
            done(ts(cnt_u[:], cm[:, 1:2], float(NE), None, ALU.add), "routed")
            blocks = v.value_load(cnt_u[0:1, 0:1], min_val=NE, max_val=NE * MAXB)

            def choose(n):
                cp(rsel[:], rhsx[:, bass.ds(n % NE, 1), :, :].rearrange("p a c w -> p (a c) w"))
                for c in range(NL):
                    last = ts(Pm[:, c, :], iota, rankb[:, c, bass.ds(n, 1)], None, ALU.is_equal)
                last.then_inc(sem("pm_ready"), 1)

            def number(n):
                v.wait_ge(sem("slots_done"), n + 1)
                ts(idx[:], ps[7][:, 0:2], NONE, None, ALU.add).then_inc(sem("idx_ready"), 1)

            v.sem_inc(sem("u_read"), 2)
            cp(rsel[:], rhsx[:, 0, :, :])
            for c in range(NL):
                last = ts(Pm[:, c, :], iota, rankb[:, c, 0:1], None, ALU.is_equal)
            last.then_inc(sem("pm_ready"), 1)
            number(0)
            with v.Fori(0, blocks) as i:
                v.wait_ge(sem("block_moved"), i + 1)
                v.wait_ge(sem("idx_ready"), i + 1)
                cp(idp[:], idx[:, 1:2]).then_inc(sem("idp_ready"), 1)
                v.wait_ge(sem("idp_ready"), i + 1)
                choose(i + 1)
                for hf in range(2):
                    v.wait_ge(sem(f"slot_free{4 * hf + 3}"), i + 2)
                    u = pall[:, 2 * hf:2 * hf + 2, :].rearrange("p b (n w) -> p b n w", w=2)
                    g3, l3 = [a[:, hf].rearrange("p (b n) -> p b n", b=2) for a in (glu, lin)]
                    ts(g3, u[:, :, :, 0], LIMIT, None, ALU.min).then_inc(sem("glu_ready"), 1)
                    ts(l3, u[:, :, :, 1], LIMIT, -LIMIT, ALU.min, ALU.max).then_inc(sem("u_read"), 1)
                    v.wait_ge(sem("glu_ready"), 2 * i + hf + 1)
                    v.wait_ge(sem("u_read"), 2 * i + hf + 3)
                    stt(lin[:, hf], lin[:, hf], 1.0, glu[:, hf], ALU.add, ALU.mult).then_inc(sem("lin_ready"), 1)
                    v.wait_ge(sem("lin_ready"), 2 * i + hf + 1)
                    v.wait_ge(sem("sg_ready"), 2 * i + hf + 1)
                    tt(actv[:, hf], lin[:, hf], sg[:, hf], ALU.mult).then_inc(sem("act_ready"), 1)
                    if hf == 0:
                        number(i + 1)
            for c in range(NL):
                v.wait_ge(sem(f"fin_in{c}"), 16)
                if c >= 2:
                    v.wait_ge(sem(f"out_done{c % 2}"), 16)
                o = fo[:, c % 2]
                done(ts(o, fin[:, c, 0], gate[:, c, 0:1], None, ALU.mult), "v_chain")
                for k in range(1, TOPK):
                    done(stt(o, fin[:, c, k], gate[:, c, k:k + 1], o, ALU.mult, ALU.add), "f_sum" if k == TOPK - 1 else "v_chain")
                mean("f", slice(c, c + 1), D, c + 1)
                done(stt(o, o, ss[:, 1, c:c + 1], gw[:, 1], ALU.mult, ALU.mult), "v_chain")
                v.wait_ge(sem("res_in"), 32)
                done(tt(o, o, fx[:, c], ALU.add), "out_ready")

        @block.gpsimd
        def _(pool):
            pool.wait_ge(sem("routed"), 1)
            blocks = pool.value_load(cnt_u[0:1, 0:1], min_val=NE, max_val=NE * MAXB)
            pool.sem_inc(sem("block_moved"), 1)

            def gather():
                pool.indirect_dma_start(xg, None, xn_d, bass.IndirectOffsetOnAxis(ap=idx[:, 0:1], axis=0),
                                        bounds_check=SEQ - 1, oob_is_err=False).then_inc(sem("xg_in"), 16)

            pool.wait_ge(sem("xn_out"), 16 * NL)
            pool.wait_ge(sem("idx_ready"), 1)
            gather()
            with pool.Fori(0, blocks) as i:
                pool.wait_ge(sem("idx_ready"), i + 2)
                pool.wait_ge(sem("xg_turned"), 2 * i + 2)
                pool.sem_inc(sem("gathering"), 1)
                gather()
                pool.wait_ge(sem("y_ready"), i + 2)
                pool.wait_ge(sem("idp_ready"), i + 1)
                pool.sem_inc(sem("scattering"), 1)
                pool.indirect_dma_start(yp_d, bass.IndirectOffsetOnAxis(ap=idp[:, 0:1], axis=0), yv, None,
                                        bounds_check=SEQ * TOPK - 1, oob_is_err=False).then_inc(sem("scattered"), 16)
                pool.wait_ge(sem("scattered"), 16 * i + 16)
                pool.wait_ge(sem("xg_in"), 16 * i + 32)
                pool.sem_inc(sem("block_moved"), 1)
            pool.sem_inc(sem("all_scattered"), 1)


def kernel(x, c, ctx, c_ctx, ada_w, ada_b, mix_pre_norm, mix_post_norm, w_in, w_out, ssd_conv_w, ssd_conv_b, ssd_dt_bias,
           ssd_a_log, ssd_d, ssd_norm, hg_lb, hg_norm, ffn_pre_norm, ffn_post_norm, router_w, router_b, moe_w1, moe_b1,
           moe_w2, moe_b2):
    import concourse.bacc as bacc
    from concourse.bass_utils import run_bass_kernel_spmd

    f = [np.asarray(a) for a in (c, c_ctx, mix_pre_norm, ffn_pre_norm, ssd_conv_w, ssd_conv_b, ada_b)]
    c_, cc_, mp, fp, cw, cb, ab = f

    def col(a):
        return np.ascontiguousarray(a.reshape(-1, P).T)

    cvec = np.stack([col(c_), col(cc_)], 2).reshape(P, 16)
    cwt = np.stack([col(cw[0, k]) for k in range(TAPS)], 2).reshape(P, 30)
    cols = np.ascontiguousarray(np.concatenate([cvec, col(mp), col(fp), cwt, col(cb), col(ab)], 1))
    ab = ab.reshape(-1)
    rows = np.concatenate([np.asarray(a).reshape(-1) for a in (
        hg_lb, ssd_norm, hg_norm, ssd_dt_bias, ssd_a_log, ssd_d, router_b, ab[2 * D:3 * D], ab[5 * D:6 * D],
        mix_post_norm, ffn_post_norm)])[None, :]
    bias = np.ascontiguousarray(np.concatenate([np.asarray(moe_b1)[0], np.asarray(moe_b2)[0]], 1))
    cf, cu = consts()
    arrays = dict(x=np.asarray(x)[0], ctx_in=np.asarray(ctx)[0], cols=cols, rows=np.ascontiguousarray(rows),
                  w_ada=np.asarray(ada_w)[0], w_in=np.asarray(w_in)[0], w_out=np.asarray(w_out)[0],
                  w_rt=np.asarray(router_w)[0], w1=np.asarray(moe_w1)[0], w2=np.asarray(moe_w2)[0], bb=bias, cf_in=cf, cu_in=cu)
    nc = bacc.Bacc("TRN2", target_bir_lowering=False, num_devices=1)
    args = {n: nc.dram_tensor(n, a.shape, mybir.dt.from_np(a.dtype), kind="ExternalInput").ap() for n, a in arrays.items()}
    out = nc.dram_tensor("out", (SEQ, D), F32, kind="ExternalOutput").ap()
    program(nc, out=out, **args)
    r = run_bass_kernel_spmd(nc, [arrays], core_ids=[0])
    return np.asarray(r.results[0]["out"]).reshape(1, SEQ, D)
```
